# Optimizing a Trainium2 kernel written in Bass

```python
import math
import jax
import jax.numpy as jnp
from jax import lax
import numpy as np

D_MODEL = 1024
BATCH = 1
SEQ = 512
DEPTH = 2

N_A_LAYERS = DEPTH // 2
N_B_LAYERS = DEPTH - N_A_LAYERS
N_HEADS = 8
A_HEAD_DIM = 64
A_QK_WIDTH = N_HEADS * 2 * A_HEAD_DIM
A_V_WIDTH = N_HEADS * 2 * A_HEAD_DIM
B_GROUPS = ((128, 1), (512, 4), (2048, 16))
B_NUM_GROUPS = len(B_GROUPS)
B_HEAD_DIM = 64
B_QK_WIDTH = B_NUM_GROUPS * N_HEADS * B_HEAD_DIM
B_OUT_WIDTH = N_HEADS * B_HEAD_DIM
Q_BLOCK = 128
REL_BUCKETS = 32
REL_MAX_EXACT = 16
REL_MAX_DIST = 2048
MOE_GROUPS = 4
MOE_EXPERTS_PER_GROUP = 8
MOE_EXPERTS = MOE_GROUPS * MOE_EXPERTS_PER_GROUP
MOE_TOP_K = 2
MOE_HIDDEN = 512
MOE_BLOCK = 128
EPS = 1e-6

kernel_name = 'hybrid_yoco_diffattn_dilated_hmoe'

def rmsnorm(t, g):
    t32 = t.astype(jnp.float32)
    y = t32 * lax.rsqrt(jnp.mean(t32 * t32, axis=-1, keepdims=True) + EPS)
    return (y * g.astype(jnp.float32)).astype(t.dtype)

def modulate(h, shift, scale):
    return h * (1 + scale[:, None, :]) + shift[:, None, :]

def t5_bucket(dist):
    n = jnp.maximum(dist, 0)
    nf = jnp.maximum(n, 1).astype(jnp.float32)
    large = REL_MAX_EXACT + (jnp.log(nf / REL_MAX_EXACT) / math.log(REL_MAX_DIST / REL_MAX_EXACT)
                             * (REL_BUCKETS - REL_MAX_EXACT)).astype(jnp.int32)
    large = jnp.minimum(large, REL_BUCKETS - 1)
    return jnp.where(n < REL_MAX_EXACT, n, large)

def lambda_init(layer):
    return 0.8 - 0.6 * math.exp(-0.3 * layer)

def diff_attention(h, w_qkv, q_gain, k_gain, lam_p, subln_gain, w_o, rel_bias, lam_init):
    b, s, _ = h.shape
    q, k, v = jnp.split(h @ w_qkv, [A_QK_WIDTH, 2 * A_QK_WIDTH], axis=-1)
    q = rmsnorm(q.reshape(b, s, N_HEADS, 2, A_HEAD_DIM), q_gain)
    k = rmsnorm(k.reshape(b, s, N_HEADS, 2, A_HEAD_DIM), k_gain)
    v = v.reshape(b, s, N_HEADS, 2 * A_HEAD_DIM)
    lp = lam_p.astype(jnp.float32)
    lam = jnp.exp(jnp.sum(lp[0] * lp[1])) - jnp.exp(jnp.sum(lp[2] * lp[3])) + lam_init
    scale = A_HEAD_DIM ** -0.5
    k_pos = jnp.arange(s)

    def block(i):
        start = i * Q_BLOCK
        q_blk = lax.dynamic_slice_in_dim(q, start, Q_BLOCK, axis=1)
        logits = jnp.einsum('bqhcd,bkhcd->bchqk', q_blk, k,
                            preferred_element_type=jnp.float32) * scale
        dist = (start + jnp.arange(Q_BLOCK))[:, None] - k_pos[None, :]
        bias = jnp.transpose(rel_bias[t5_bucket(dist)], (2, 0, 1)).astype(jnp.float32)
        logits = jnp.where(dist >= 0, logits + bias, -jnp.inf)
        p = jax.nn.softmax(logits, axis=-1)
        attn = p[:, 0] - lam * p[:, 1]
        return jnp.einsum('bhqk,bkhe->bqhe', attn.astype(v.dtype), v)

    o = lax.map(block, jnp.arange(s // Q_BLOCK))
    o = jnp.moveaxis(o, 0, 1).reshape(b, s, N_HEADS, 2 * A_HEAD_DIM)
    o = rmsnorm(o, subln_gain) * (1 - lam_init)
    return o.reshape(b, s, A_V_WIDTH) @ w_o

def _to_subseq(t, dil):
    b, s = t.shape[:2]
    rest = t.shape[2:]
    length = s // dil
    t = jnp.swapaxes(t.reshape((b, length, dil) + rest), 1, 2).reshape((b * dil, length) + rest)
    lp = -(-length // Q_BLOCK) * Q_BLOCK
    return jnp.pad(t, [(0, 0), (0, lp - length)] + [(0, 0)] * len(rest))

def _from_subseq(t, b, s, dil):
    length = s // dil
    rest = t.shape[2:]
    t = t[:, :length].reshape((b, dil, length) + rest)
    return jnp.swapaxes(t, 1, 2).reshape((b, s) + rest)

def _key_blocks(t):
    bp, lp = t.shape[:2]
    rest = t.shape[2:]
    nb = lp // Q_BLOCK
    tp = jnp.pad(t, [(0, 0), (Q_BLOCK, 0)] + [(0, 0)] * len(rest))
    prev = tp[:, :lp].reshape((bp, nb, Q_BLOCK) + rest)
    cur = tp[:, Q_BLOCK:].reshape((bp, nb, Q_BLOCK) + rest)
    return jnp.concatenate([prev, cur], axis=2)

def _band_bias_mask(band, dil, nb, rel_bias):
    i = jnp.arange(Q_BLOCK)[:, None]
    j = jnp.arange(2 * Q_BLOCK)[None, :]
    rel = i + Q_BLOCK - j
    key_idx = jnp.arange(nb)[:, None, None] * Q_BLOCK + j[None] - Q_BLOCK
    mask = (rel >= 0)[None] & (rel <= band)[None] & (key_idx >= 0)
    bias = jnp.transpose(rel_bias[t5_bucket(dil * rel)], (2, 0, 1)).astype(jnp.float32)
    return bias, mask

def shared_dilated_kv(x, c_act, kv_norm, kv_ada_w, kv_ada_b, kv_w, kv_k_norm):
    b, s, _ = x.shape
    shift, scale = jnp.split(c_act @ kv_ada_w + kv_ada_b, 2, axis=-1)
    h = modulate(rmsnorm(x, kv_norm), shift, scale)
    k, v = jnp.split(h @ kv_w, 2, axis=-1)
    k = rmsnorm(k.reshape(b, s, B_NUM_GROUPS, N_HEADS, B_HEAD_DIM), kv_k_norm[:, None, :])
    v = v.reshape(b, s, B_NUM_GROUPS, N_HEADS, B_HEAD_DIM)
    blocks = []
    for g, (_, dil) in enumerate(B_GROUPS):
        blocks.append((_key_blocks(_to_subseq(k[:, :, g], dil)),
                       _key_blocks(_to_subseq(v[:, :, g], dil))))
    return blocks

def dilated_attention(h, w_q, q_gain, w_o, kv_blocks, rel_bias):
    b, s, _ = h.shape
    q = rmsnorm((h @ w_q).reshape(b, s, B_NUM_GROUPS, N_HEADS, B_HEAD_DIM), q_gain[:, None, :])
    scale = B_HEAD_DIM ** -0.5
    outs, lses = [], []
    for g, (window, dil) in enumerate(B_GROUPS):
        kb, vb = kv_blocks[g]
        bp, nb = kb.shape[:2]
        qb = _to_subseq(q[:, :, g], dil).reshape(bp, nb, Q_BLOCK, N_HEADS, B_HEAD_DIM)
        bias, mask = _band_bias_mask(window // dil, dil, nb, rel_bias)
        logits = jnp.einsum('bnqhd,bnkhd->bnhqk', qb, kb,
                            preferred_element_type=jnp.float32) * scale
        logits = jnp.where(mask[None, :, None], logits + bias[None, None], -jnp.inf)
        lse = jax.nn.logsumexp(logits, axis=-1)
        p = jnp.exp(logits - lse[..., None])
        o = jnp.einsum('bnhqk,bnkhd->bnqhd', p.astype(vb.dtype), vb)
        outs.append(_from_subseq(o.reshape(bp, nb * Q_BLOCK, N_HEADS, B_HEAD_DIM), b, s, dil))
        lses.append(_from_subseq(jnp.swapaxes(lse, 2, 3).reshape(bp, nb * Q_BLOCK, N_HEADS), b, s, dil))
    w = jax.nn.softmax(jnp.stack(lses, axis=2), axis=2)
    o = jnp.einsum('bsgh,bsghd->bshd', w.astype(outs[0].dtype), jnp.stack(outs, axis=2))
    return o.reshape(b, s, B_OUT_WIDTH) @ w_o

def hier_moe(h, w_group, b_group, w_expert, b_expert, w_gate, w_up, w_down):
    t = h.shape[0]
    g_logits = (h @ w_group).astype(jnp.float32) + b_group.astype(jnp.float32)
    g_idx = jnp.argmax(g_logits, axis=-1)
    g_w = jnp.take_along_axis(jax.nn.softmax(g_logits, axis=-1), g_idx[:, None], axis=1)
    e_logits = ((h @ w_expert).astype(jnp.float32) + b_expert.astype(jnp.float32)).reshape(
        t, MOE_GROUPS, MOE_EXPERTS_PER_GROUP)
    e_sel = jnp.take_along_axis(e_logits, g_idx[:, None, None], axis=1)[:, 0]
    top_v, top_i = lax.top_k(e_sel, MOE_TOP_K)
    gates = g_w * jax.nn.softmax(top_v, axis=-1)
    eid = (g_idx[:, None] * MOE_EXPERTS_PER_GROUP + top_i).reshape(-1)
    tok = jnp.repeat(jnp.arange(t), MOE_TOP_K)
    wts = gates.reshape(-1)
    n_assign = t * MOE_TOP_K
    order = jnp.argsort(eid)
    eid_s, tok_s, wts_s = eid[order], tok[order], wts[order]
    counts = jax.ops.segment_sum(jnp.ones_like(eid_s), eid_s, num_segments=MOE_EXPERTS)
    starts = jnp.cumsum(counts) - counts
    padded = (counts + MOE_BLOCK - 1) // MOE_BLOCK * MOE_BLOCK
    pad_end = jnp.cumsum(padded)
    pad_start = pad_end - padded
    dest = pad_start[eid_s] + jnp.arange(n_assign) - starts[eid_s]
    n_blocks = -(-n_assign // MOE_BLOCK) + MOE_EXPERTS
    rows = n_blocks * MOE_BLOCK
    row_tok = jnp.zeros((rows,), jnp.int32).at[dest].set(tok_s)
    row_w = jnp.zeros((rows,), jnp.float32).at[dest].set(wts_s)
    block_e = jnp.minimum(jnp.searchsorted(pad_end, jnp.arange(n_blocks) * MOE_BLOCK, side='right'),
                          MOE_EXPERTS - 1)
    xs = h[row_tok].reshape(n_blocks, MOE_BLOCK, h.shape[1])

    def expert_block(args):
        xb, e = args
        return (jax.nn.silu(xb @ w_gate[e]) * (xb @ w_up[e])) @ w_down[e]

    ys = lax.map(expert_block, (xs, block_e)).reshape(rows, h.shape[1])
    return jnp.zeros_like(h).at[row_tok].add(ys * row_w[:, None].astype(h.dtype))

def setup_inputs(seed: int = 0) -> dict:
    key = jax.random.key(seed)
    ks = jax.random.split(key, 28)
    D = D_MODEL

    def nrm(k, shape, scale):
        return jax.random.normal(k, shape, jnp.float32) * scale

    def gain(k, shape):
        return 1.0 + 0.02 * jax.random.normal(k, shape, jnp.float32)

    return {
        'x': nrm(ks[0], (BATCH, SEQ, D), 1.0),
        'c': nrm(ks[1], (BATCH, D), 1.0),
        'rel_bias': nrm(ks[2], (REL_BUCKETS, N_HEADS), 0.5),
        'ada_w': nrm(ks[3], (DEPTH, D, 6 * D), 0.02),
        'ada_b': nrm(ks[4], (DEPTH, 6 * D), 0.02),
        'norm_attn': gain(ks[5], (DEPTH, D)),
        'norm_ffn': gain(ks[6], (DEPTH, D)),
        'a_w_qkv': nrm(ks[7], (N_A_LAYERS, D, 2 * A_QK_WIDTH + A_V_WIDTH), D ** -0.5),
        'a_q_norm': gain(ks[8], (N_A_LAYERS, A_HEAD_DIM)),
        'a_k_norm': gain(ks[9], (N_A_LAYERS, A_HEAD_DIM)),
        'a_lambda': nrm(ks[10], (N_A_LAYERS, 4, A_HEAD_DIM), 0.1),
        'a_subln': gain(ks[11], (N_A_LAYERS, 2 * A_HEAD_DIM)),
        'a_w_o': nrm(ks[12], (N_A_LAYERS, A_V_WIDTH, D), A_V_WIDTH ** -0.5),
        'kv_norm': gain(ks[13], (D,)),
        'kv_ada_w': nrm(ks[14], (D, 2 * D), 0.02),
        'kv_ada_b': nrm(ks[15], (2 * D,), 0.02),
        'kv_w': nrm(ks[16], (D, 2 * B_QK_WIDTH), D ** -0.5),
        'kv_k_norm': gain(ks[17], (B_NUM_GROUPS, B_HEAD_DIM)),
        'b_w_q': nrm(ks[18], (N_B_LAYERS, D, B_QK_WIDTH), D ** -0.5),
        'b_q_norm': gain(ks[19], (N_B_LAYERS, B_NUM_GROUPS, B_HEAD_DIM)),
        'b_w_o': nrm(ks[20], (N_B_LAYERS, B_OUT_WIDTH, D), B_OUT_WIDTH ** -0.5),
        'moe_w_group': nrm(ks[21], (DEPTH, D, MOE_GROUPS), D ** -0.5),
        'moe_b_group': nrm(ks[22], (DEPTH, MOE_GROUPS), 0.01),
        'moe_w_expert': nrm(ks[23], (DEPTH, D, MOE_EXPERTS), D ** -0.5),
        'moe_b_expert': nrm(ks[24], (DEPTH, MOE_EXPERTS), 0.01),
        'moe_w_gate': nrm(ks[25], (DEPTH, MOE_EXPERTS, D, MOE_HIDDEN), D ** -0.5),
        'moe_w_up': nrm(ks[26], (DEPTH, MOE_EXPERTS, D, MOE_HIDDEN), D ** -0.5),
        'moe_w_down': nrm(ks[27], (DEPTH, MOE_EXPERTS, MOE_HIDDEN, D), MOE_HIDDEN ** -0.5),
    }

def reference(x, c, rel_bias, ada_w, ada_b, norm_attn, norm_ffn, a_w_qkv, a_q_norm, a_k_norm,
              a_lambda, a_subln, a_w_o, kv_norm, kv_ada_w, kv_ada_b, kv_w, kv_k_norm,
              b_w_q, b_q_norm, b_w_o, moe_w_group, moe_b_group, moe_w_expert, moe_b_expert,
              moe_w_gate, moe_w_up, moe_w_down):
    b, s, d = x.shape
    c_act = jax.nn.silu(c)
    kv_blocks = None
    for layer in range(DEPTH):
        mod = c_act @ ada_w[layer] + ada_b[layer]
        sh_a, sc_a, g_a, sh_f, sc_f, g_f = jnp.split(mod, 6, axis=-1)
        h = modulate(rmsnorm(x, norm_attn[layer]), sh_a, sc_a)
        if layer < N_A_LAYERS:
            y = diff_attention(h, a_w_qkv[layer], a_q_norm[layer], a_k_norm[layer], a_lambda[layer],
                               a_subln[layer], a_w_o[layer], rel_bias, lambda_init(layer))
        else:
            if layer == N_A_LAYERS:
                kv_blocks = shared_dilated_kv(x, c_act, kv_norm, kv_ada_w, kv_ada_b, kv_w, kv_k_norm)
            j = layer - N_A_LAYERS
            y = dilated_attention(h, b_w_q[j], b_q_norm[j], b_w_o[j], kv_blocks, rel_bias)
        x = x + g_a[:, None, :] * y
        h = modulate(rmsnorm(x, norm_ffn[layer]), sh_f, sc_f)
        y = hier_moe(h.reshape(b * s, d), moe_w_group[layer], moe_b_group[layer], moe_w_expert[layer],
                     moe_b_expert[layer], moe_w_gate[layer], moe_w_up[layer], moe_w_down[layer])
        x = x + g_f[:, None, :] * y.reshape(b, s, d)
    return x


_drawn_inputs = setup_inputs


def setup_inputs(seed=0):
    import zlib

    import numpy as np

    out = dict(_drawn_inputs(seed))
    spreads = {}
    factors = {'norm_attn': 7.802,
     'a_q_norm': 8.0,
     'a_k_norm': 6.35,
     'a_subln': 3.907,
     'kv_norm': 8.0,
     'kv_ada_b': 6.49,
     'kv_k_norm': 8.0,
     'b_q_norm': 8.0,
     'moe_b_group': 3.868,
     'moe_b_expert': 5.536}
    for name, (base, spread) in spreads.items():
        noise = np.random.default_rng([zlib.crc32(name.encode()), seed]).standard_normal(out[name].shape)
        drawn = base * np.exp(spread * noise) if base else spread * noise
        out[name] = jnp.asarray(drawn.astype(out[name].dtype))
    for name, factor in factors.items():
        out[name] = (out[name] * factor).astype(out[name].dtype)
    return out
```

```python
import math
from contextlib import ExitStack

import numpy as np

import concourse.bass as bass
from concourse import mybir

F32 = mybir.dt.float32
BF16 = mybir.dt.bfloat16
I32 = mybir.dt.int32
ALU = mybir.AluOpType
ACT = mybir.ActivationFunctionType
AX = mybir.AxisListType
ds = bass.ds

P = 128
D = 1024
S = 512
LAYERS = 2
KC = D // P
TC = S // P
H = 8
DH = 64
GROUPS = 3
BUCKETS, MAX_EXACT, MAX_DIST = 32, 16, 2048
NG, PER_G, E, HID = 4, 8, 32, 512
NR = NG + E
EPS = 1e-6
LAM_INIT = 0.8 - 0.6 * math.exp(-0.3 * 0)
NEG = -1e30
RING = 6
HALF = 512
UNUSED = 4096
CREDIT = 4
FDIST = S + P

C_ID, C_TRI, C_ONE = 0, 128, 256
C_E512, C_IE, C_IG, C_AID = 384, 416, 448, 452
C_END = 460
M_BAND, M_4, M_16, M_END = 0, 256, 768, 1280
M_FLIP = M_END

V_C, V_NA, V_NF, V_KN, V_KAB = 0, 8, 24, 40, 48
V_QG, V_KG, V_SUB, V_BQ, V_BQ2, V_BK, V_BK2 = 64, 65, 66, 67, 68, 69, 70
V_END = 71

BLOCKS = {0: [("mod", 4), ("qkv", 6), ("gates", 8), ("wo", 2)],
          1: [("kvmod", 4), ("kv", 6), ("mod", 4), ("q", 3), ("gates", 8), ("wo", 1)]}
MOE_BLOCKS = 3 * E


def block_starts():
    at, out = 0, {}
    for layer in range(LAYERS):
        for kind, n in BLOCKS[layer]:
            out[layer, kind] = at
            at += n
        out[layer, "moe"] = at
        at += MOE_BLOCKS
    return out


START = block_starts()


def bucket_table():
    dist = (S - 1) - np.arange(FDIST)
    n = np.maximum(dist, 0)
    nf = np.maximum(n, 1).astype(np.float32)
    large = MAX_EXACT + (np.log(nf / MAX_EXACT) / math.log(MAX_DIST / MAX_EXACT)
                         * (BUCKETS - MAX_EXACT)).astype(np.int32)
    bucket = np.where(n < MAX_EXACT, n, np.minimum(large, BUCKETS - 1))
    out = np.zeros((BUCKETS + 1, FDIST), np.float32)
    out[bucket, np.arange(FDIST)] = (dist >= 0)
    out[BUCKETS] = (dist < 0)
    return out


def constants():
    p = np.arange(P)[:, None]
    c = np.zeros((P, C_END), np.float32)
    c[:, C_ID:C_ID + P] = np.eye(P)
    c[:, C_TRI:C_TRI + P] = p < np.arange(P)[None, :]
    c[:, C_ONE:C_ONE + P] = 1.0
    c[:, C_E512:C_E512 + E] = S * np.arange(E)
    c[:, C_IE:C_IE + E] = np.arange(E) - 64
    c[:, C_IG:C_IG + NG] = np.arange(NG) - 64
    c[:, C_AID:C_AID + 2 * TC] = p + P * np.arange(2 * TC)
    m = np.zeros((P, M_END + P), np.float32)
    m[:, M_FLIP:M_FLIP + P] = np.eye(P)[::-1]
    m[:, M_BAND:M_4][p + P - np.arange(2 * P)[None, :] > P] = NEG
    for at, dil in ((M_4, 4), (M_16, 16)):
        m[:, at:at + S][(p + 3 * P - np.arange(S)[None, :]) % dil != 0] = NEG
    return c, m


class Steps:

    def __init__(self, eng, sem):
        self.eng, self.sem, self.base, self.n, self.it, self.per = eng, sem, 0, 0, 0, 0

    def __call__(self, ins):
        ins.then_inc(self.sem, 1)
        self.n += 1
        self.eng.wait_ge(self.sem, self.it * self.per + (self.base + self.n))

    def enter(self, it, per):
        self.base, self.n, self.it, self.per = self.base + self.n, 0, it, per

    def leave(self, times):
        assert self.n == self.per, (self.n, self.per)
        self.base, self.n, self.it, self.per = self.base + self.per * times, 0, 0, 0


class Signal:

    def __init__(self, sem, base):
        self.sem, self.base = sem, base

    def __call__(self, value):
        return self.sem, value + self.base


def program(nc, t, const, masks, buckets, out):
    with ExitStack() as ctx:
        def sb(name, shape, dt=F32):
            return ctx.enter_context(nc.sbuf_tensor(name, shape, dt))

        def sem(name):
            return ctx.enter_context(nc.semaphore(name))

        def dram(name, shape, dt=F32):
            return nc.dram_tensor(name, shape, dt, kind="Internal").ap()

        ring = sb("ring", [P, RING, KC * HALF])
        X = sb("X", [P, TC * D])
        XN = sb("XN", [P, TC * D])
        HT = sb("HT", [P, KC * S])
        T = sb("T", [P, H * S])
        V = sb("V", [P, TC * GROUPS * HALF])
        W = sb("W", [P, 3840])
        C = sb("C", [P, C_END])
        maskb = sb("maskb", [P, M_END], BF16)
        identb = sb("identb", [P, P], BF16)
        colA = sb("colA", [P, LAYERS * 48])
        colV = sb("colV", [P, V_END])
        cact = sb("cact", [P, KC])
        mod = sb("mod", [P, 48])
        kvm = sb("kvm", [P, 16])
        scl = sb("scl", [P, 3, KC])
        lamw = sb("lamw", [P, 8])
        nlam = sb("nlam", [P, 1])
        rw = sb("rw", [P, KC * NR])
        rbias = sb("rbias", [P, NR])
        small = sb("small", [P, 48])
        small2 = sb("small2", [P, 40])
        gates = sb("gates", [P, 2, TC])
        dest = sb("dest", [P, 2 * TC], I32)
        aid = sb("aid", [P, 2 * TC], I32)
        tokc, dstc = sb("tokc", [P, 2], I32), sb("dstc", [P, 2], I32)
        pause = sb("pause", [P, 1])
        flag = sb("flag", [P, 1], I32)
        tok = sb("tok", [P, TC * E], I32)
        dst = sb("dst", [P, TC * E], I32)
        bank = [ctx.enter_context(nc.psum_tensor(f"bank{i}", [P, 512], F32)) for i in range(8)]

        ident, flip = C[:, C_ID:C_ID + P], V[:, 5376:5376 + P]
        tri, ones = C[:, C_TRI:C_TRI + P], C[:, C_ONE:C_ONE + P]
        x3 = X[:, :].rearrange("p (c n) -> p c n", c=TC)
        xn3 = XN[:, :].rearrange("p (c n) -> p c n", c=TC)
        ht3 = HT[:, :].rearrange("p (k s) -> p k s", k=KC)
        rw3 = rw[:, :].rearrange("p (k n) -> p k n", k=KC)
        vw = [D, GROUPS * HALF]
        val = [V[:, 0:TC * w].rearrange("p (c n) -> p c n", c=TC) for w in vw]

        qw = [D, GROUPS * HALF]
        q_d = [dram(f"q_scratch{l}", [S, qw[l]]) for l in range(LAYERS)]
        k_d = [dram(f"k_scratch{l}", [S, qw[l]]) for l in range(LAYERS)]
        fb_d = dram("bias_scratch", [H, FDIST])
        gate_d = [dram(f"gate_scratch{l}", [16, P]) for l in range(LAYERS)]
        xn_d = [dram(f"xn_scratch{l}", [S, D]) for l in range(LAYERS)]
        x1_d = dram("x1_scratch", [S, D])
        tab_d = [dram(f"slot_table{l}", [E * S, 1], I32) for l in range(LAYERS)]
        ys_d = [dram(f"expert_rows{l}", [2 * S, D]) for l in range(LAYERS)]

        w_in = [sem(f"w_in{i}") for i in range(RING)]
        w_used = sem("w_used")
        const_in, x_in, vec_in, bias_in = sem("const_in"), sem("x_in"), sem("vec_in"), sem("bias_in")
        tab_in = sem("tab_in")
        setup_pe, setup_dve, setup_act = sem("setup_pe"), sem("setup_dve"), sem("setup_act")
        fb_out, hank_in = sem("fb_out"), sem("hank_in")
        dve_s, act_s, pool_s = sem("dve_step"), sem("act_step"), sem("pool_step")
        out_done = sem("out_done")
        PROJ = {0: [("q", 0), ("q", 1), ("k", 0), ("k", 1), ("v", 0), ("v", 1)],
                1: [("k", 0), ("k", 1), ("k", 2), ("v", 0), ("v", 1), ("v", 2), ("q", 0), ("q", 1), ("q", 2)]}
        PHASES = {0: [("qkv", 0, 6)], 1: [("kv", 0, 6), ("q", 6, 9)]}

        def staged_before(l, j):
            return TC * sum(kind != "v" for kind, _ in PROJ[l][:j])

        N_STAGED = [staged_before(l, len(PROJ[l])) for l in range(LAYERS)]
        counts = dict(
            mod_pe=1, mod_ready=2, gate_pe=2, gate_rows=1, gate_out=32,
            ss_ready=TC, rms_arg=1, rms_root=1, xn_ready=TC, xt_pe=KC, ht_ready=KC,
            proj_pe=6 * TC, proj_free=6 * TC, sq_ready=4 * TC, q_arg=4 * TC, q_root=4 * TC, stage_ready=4 * TC,
            qk_pe=QK_CREDIT[0] + H * QK_STEPS[0], qk_t=H * QK_STEPS[0],
            s_pe=CREDIT + H * TC, logits=CREDIT + H * TC, exps=2 * H * TC, probs=H * TC,
            pt_pe=H * TC, pt=H * TC, o_pe=CREDIT + H * TC, o_out=CREDIT + H * TC,
            sub_sq=TC, sub_arg=TC + 1, sub_root=1, sub_ready=TC, ot_pe=KC, ot_ready=KC,
            wo_pe=2 * TC, y_added=2 * TC, ga_in=16, x_re_in=16, gf_in=16,
            ss2=TC, arg2=1, root2=1, xn2=TC, xt2_pe=KC, ht2=KC, xn_out=16,
            rw_in=64, route_pe=1, route_e=2, route_e_done=2, picked=1, rank_pe=1, dest_ready=1,
            tab_scat=16 * 2 * TC, tab_back=16, tab_f=1, tab_pe=1, tok_ready=1, flag_ready=1, g_zero=1,
            xr_pe=2 * E, xr_t=2 * E, gu_pe=2 * E, silu=E, hid=E, hid_pe=CREDIT + E, hid_t=E, dn_pe=2 * E,
            y_evac=2 * E, scat_all=1, comb_free=TC, x_new=TC, x_out=16 * TC)
        pairs = dict(stage_out=16 * N_STAGED[0] // 2, stage_in=H // 2 * STAGE_DMAS[0],
                     gath=16 * E // 2, scat=16 * E // 2, rows_in=16 * TC // 2)
        sems = {n: sem(n) for n in counts}
        sems2 = {n: [sem(f"{n}{i}") for i in range(2)] for n in pairs}
        from_one = ["qk_t", "pt", "hid", "hid_t", "y_evac", "s_pe"]
        sm = [dict(**{n: Signal(sems[n], l * k + (n in from_one)) for n, k in counts.items()},
                              **{n: [Signal(x, l * k) for x in sems2[n]] for n, k in pairs.items()})
              for l in range(LAYERS)]
        ov_from_one = ["dn_pe", "xr_pe", "xr_t"]
        ov_names = ["w", "g", "xr_pe", "xr_t", "gu_pe", "silu", "hid", "hid_pe", "hid_t", "dn_pe", "y", "scat", "step"]
        ov = [dict(**{n: Signal(sem(f"ov_{n}_{l}"), int(n in ov_from_one)) for n in ov_names})
              for l in range(LAYERS)]

        def slot(n):
            return ring[:, n % RING, :]

        def slot3(n, k=KC):
            return slot(n).rearrange("p (k m) -> p k m", k=k)

        def arrived(eng, n, turn=0):
            eng.wait_ge(w_in[n % RING], turn * 16 + 16 * (n // RING + 1))

        def widths(l, c):
            return [(c + 1) * P] if l == 0 else [P * min(c + 1, 2), (c + 1) * P, (c + 1) * P]

        def expert_weights(l, e):
            g = t["moe_w_gate"][l, ds(e, 1)].rearrange("o (k p) n -> p (o k) n", p=P)
            u = t["moe_w_up"][l, ds(e, 1)].rearrange("o (k p) n -> p (o k) n", p=P)
            d = t["moe_w_down"][l, ds(e, 1)].rearrange("o (k p) n -> p (o k) n", p=P)
            return g, u, d

        n_norm = [1, 2]

        block = ctx.enter_context(nc.Block())

        @block.sync
        def _(sp):
            def load(n, src, k=KC, turn=None):
                if turn is not None:
                    sp.wait_ge(w_used, turn * RING + (n - RING + 1))
                elif n >= RING:
                    sp.wait_ge(w_used, n - RING + 1)
                sp.dma_start(slot3(n, k), src).then_inc(w_in[n % RING], 16)

            def columns(w, b):
                return w[:, b * HALF:(b + 1) * HALF].rearrange("(k p) n -> p k n", p=P)

            for l in range(LAYERS):
                src = {"mod": (t["ada_w"][l], [0, 1, 2, 3]), "gates": (t["ada_w"][l], range(4, 12)),
                       "qkv": (t["a_w_qkv"][0], range(6)), "wo": (t["a_w_o"][0], range(2)),
                       "kvmod": (t["kv_ada_w"], range(4)), "kv": (t["kv_w"], range(6)),
                       "q": (t["b_w_q"][0], range(3))}
                for kind, n in BLOCKS[l]:
                    for i in range(n):
                        if l == 1 and kind == "wo":
                            load(START[l, kind], t["b_w_o"][0].rearrange("(k p) n -> p k n", p=P), k=4)
                        else:
                            w, cols = src[kind]
                            load(START[l, kind] + i, columns(w, cols[i]))
                m = START[l, "moe"]
                g, u, _ = expert_weights(l, 0)
                load(m, g)
                load(m + 1, u)
                with sp.Fori(0, 15) as it:
                    for j in range(2):
                        g, u, _ = expert_weights(l, it * 2 + (j + 1))
                        _, _, d = expert_weights(l, it * 2 + j)
                        load(m + 2 + 3 * j, g, turn=it)
                        load(m + 3 + 3 * j, u, turn=it)
                        load(m + 4 + 3 * j, d, k=4, turn=it)
                g, u, _ = expert_weights(l, E - 1)
                load(m + 92, g)
                load(m + 93, u)
                load(m + 94, expert_weights(l, E - 2)[2], k=4)
                load(m + 95, expert_weights(l, E - 1)[2], k=4)
                sp.wait_ge(*sm[l]["flag_ready"](1))
                most = sp.value_load(flag[0:1, 0:1], min_val=0, max_val=S)
                with sp.If(most > P):
                    sp.wait_ge(w_used, m + MOE_BLOCKS)
                    for b in range(1, TC):
                        with sp.Fori(0, E) as e:
                            u0 = (b - 1) * E
                            g, u, d = expert_weights(l, e)
                            sp.wait_ge(*ov[l]["dn_pe"](e + u0))
                            sp.dma_start(slot3(0), g).then_inc(ov[l]["w"].sem, 16)
                            sp.dma_start(slot3(1), u).then_inc(ov[l]["w"].sem, 16)
                            sp.dma_start(slot3(2, 4), d).then_inc(ov[l]["w"].sem, 16)
                    sp.wait_ge(*ov[l]["dn_pe"]((TC - 1) * E))
            for c in range(TC):
                sp.wait_ge(*sm[1]["x_new"](c + 1))
                sp.dma_start(out[0, c * P:(c + 1) * P, :], x3[:, c, :]).then_inc(out_done, 16)
            sp.wait_ge(out_done, 16 * TC)

        @block.gpsimd
        def _(pool):
            step = Steps(pool, pool_s)
            for n in from_one:
                pool.sem_inc(sems[n], 1)
            for o in ov:
                for sig in (o["dn_pe"], o["xr_pe"], o["xr_t"]):
                    pool.sem_inc(sig.sem, 1)
            empty = V[:, 5120:5120 + P].bitcast(I32)
            step(pool.memset(empty, UNUSED))
            for l in range(LAYERS):
                pool.dma_start(tab_d[l].rearrange("(p n) o -> p (n o)", p=P), empty).then_inc(tab_in, 16)
            pool.wait_ge(setup_dve, 5)
            pool.dma_start(fb_d, W[0:H, 1024:1024 + FDIST]).then_inc(fb_out, 16)
            pool.wait_ge(fb_out, 16)
            hankel = bass.AP(fb_d.tensor, 0, [[1, P], [FDIST, H], [1, S]])
            pool.dma_start(V[:, 0:H * S].rearrange("p (h s) -> p h s", h=H), hankel).then_inc(hank_in, 16)

            for l in range(LAYERS):
                s, o = sm[l], ov[l]
                j = 0
                for kind, b in PROJ[l]:
                    if kind == "v":
                        continue
                    for c in range(TC):
                        pool.wait_ge(*s["stage_ready"](j + 1))
                        to = (q_d if kind == "q" else k_d)[l][c * P:(c + 1) * P, b * HALF:(b + 1) * HALF]
                        pool.dma_start(to, W[:, 1024 + HALF * (j % 2):1024 + HALF * (j % 2 + 1)]).then_inc(s["stage_out"][j % 2].sem, 16)
                        j += 1
                pool.wait_ge(*s["gate_rows"](1))
                for i in range(2):
                    pool.dma_start(gate_d[l][i * KC:(i + 1) * KC, :],
                                   W[0:KC, 3584 + i * P:3584 + (i + 1) * P]).then_inc(s["gate_out"].sem, 16)
                for i in range(2):
                    pool.wait_ge(*s["stage_out"][i](16 * (N_STAGED[l] // 2)))
                hw = P if l == 0 else GROUPS * DH
                with pool.Fori(0, H // 2) as it:
                    for b in range(2):
                        h = it * 2 + b
                        pool.wait_ge(*s["qk_pe"](it * 2 * QK_STEPS[l] + ((b - 1) * QK_STEPS[l] + QK_CREDIT[l])))
                        for i, d in enumerate((q_d[l], k_d[l])):
                            to = HT[:, (2 * b + i) * 768:(2 * b + i) * 768 + TC * hw]
                            if l == 0:
                                pool.dma_start(to.rearrange("p (c n) -> p c n", c=TC),
                                               d[:, ds(h * P, P)].rearrange("(c p) n -> p c n", p=P)).then_inc(s["stage_in"][b].sem, 16)
                            else:
                                for c in range(TC):
                                    pool.dma_start(
                                        to.rearrange("p (c g n) -> p c g n", c=TC, g=GROUPS)[:, c],
                                        d.rearrange("(c p) (g n) -> c p g n", p=P, g=GROUPS)[
                                            c, :, :, ds(h * DH, DH)]).then_inc(s["stage_in"][b].sem, 16)
                pool.wait_ge(*s["s_pe"](CREDIT + TC * H))
                xin = t["x"][0] if l == 0 else x1_d
                pool.dma_start(x3, xin.rearrange("(c p) n -> p c n", p=P)).then_inc(s["x_re_in"].sem, 16)
                pool.wait_ge(*s["o_pe"](CREDIT + TC * H))
                pool.wait_ge(*s["gate_out"](32))
                pool.dma_start(V[:, 0:D], gate_d[l][0:KC, :].rearrange("(o k) n -> o (k n)", o=1)
                               .broadcast_to([P, D])).then_inc(s["ga_in"].sem, 16)
                pool.dma_start(rw3[:, :, 0:NG], t["moe_w_group"][l].rearrange("(k p) n -> p k n", p=P)).then_inc(s["rw_in"].sem, 16)
                pool.dma_start(rw3[:, :, NG:NR], t["moe_w_expert"][l].rearrange("(k p) n -> p k n", p=P)).then_inc(s["rw_in"].sem, 16)
                pool.dma_start(rbias[:, 0:NG], t["moe_b_group"][l:l + 1, :].broadcast_to([P, NG])).then_inc(s["rw_in"].sem, 16)
                pool.dma_start(rbias[:, NG:NR], t["moe_b_expert"][l:l + 1, :].broadcast_to([P, E])).then_inc(s["rw_in"].sem, 16)
                pool.wait_ge(*s["xn2"](TC))
                pool.dma_start(xn_d[l].rearrange("(c p) n -> p c n", p=P), xn3).then_inc(s["xn_out"].sem, 16)
                pool.wait_ge(*s["y_added"](2 * TC))
                pool.memset(V[:, 0:2 * D], 0.0).then_inc(s["g_zero"].sem, 1)
                pool.wait_ge(tab_in, 32)
                pool.wait_ge(*s["dest_ready"](1))
                for j in range(2 * TC):
                    pool.indirect_dma_start(tab_d[l], bass.IndirectOffsetOnAxis(ap=dest[:, j:j + 1], axis=0),
                                            aid[:, j:j + 1], None, bounds_check=E * S - 1,
                                            oob_is_err=False).then_inc(s["tab_scat"].sem, 16)
                pool.wait_ge(*s["tab_scat"](16 * 2 * TC))
                pool.dma_start(W[0:E, 3072:3072 + S].bitcast(I32),
                               tab_d[l].rearrange("(e n) o -> e (n o)", e=E)).then_inc(s["tab_back"].sem, 16)
                pool.wait_ge(*s["tok_ready"](1))
                pool.dma_start(W[:, 0:D], gate_d[l][KC:2 * KC, :].rearrange("(o k) n -> o (k n)", o=1)
                               .broadcast_to([P, D])).then_inc(s["gf_in"].sem, 16)
                pool.wait_ge(*s["xn_out"](16))
                pool.wait_ge(*s["g_zero"](1))

                last_token, last_row = pool.to_reg(S - 1), pool.to_reg(2 * S - 1)

                def gather(col, b, signal):
                    step(pool.tensor_copy(tokc[:, b:b + 1], tok[:, ds(col, 1)]))
                    pool.tensor_tensor(pause[:, :], C[:, 0:1], C[:, 1:2], ALU.add)
                    pool.indirect_dma_start(V[:, b * D:(b + 1) * D], None, xn_d[l],
                                            bass.IndirectOffsetOnAxis(ap=tokc[:, b:b + 1], axis=0),
                                            bounds_check=last_token, oob_is_err=False).then_inc(signal, 16)

                def scatter(col, b, signal):
                    step(pool.tensor_copy(dstc[:, b:b + 1], dst[:, ds(col, 1)]))
                    pool.tensor_tensor(pause[:, :], C[:, 0:1], C[:, 1:2], ALU.add)
                    pool.indirect_dma_start(ys_d[l], bass.IndirectOffsetOnAxis(ap=dstc[:, b:b + 1], axis=0),
                                            HT[:, b * D:(b + 1) * D], None,
                                            bounds_check=last_row, oob_is_err=False).then_inc(signal, 16)

                gather(0, 0, s["gath"][0].sem)
                gather(1, 1, s["gath"][1].sem)

                def expert(e, b, more):
                    if more:
                        pool.wait_ge(*s["xr_pe"](e * 2 + 2))
                        gather(e + 2, b, s["gath"][b].sem)
                    pool.wait_ge(*s["y_evac"](e * 2 + 2))
                    scatter(e, b, s["scat"][b].sem)

                with pool.Fori(0, 15) as it:
                    step.enter(it, 4)
                    for b in range(2):
                        expert(it * 2 + b, b, True)
                    step.leave(15)
                for b in range(2):
                    expert(E - 2 + b, b, False)
                for b in range(2):
                    pool.wait_ge(*s["scat"][b](16 * (E // 2)))
                most = pool.value_load(flag[0:1, 0:1], min_val=0, max_val=S)
                with pool.If(most > P):
                    main_step, step = step, Steps(pool, o["step"].sem)
                    for b in range(1, TC):
                        with pool.Fori(0, E) as e:
                            step.enter(e, 2)
                            u0 = (b - 1) * E
                            pool.wait_ge(*o["xr_pe"](e * 2 + 2 * u0))
                            gather(e + b * E, 0, o["g"].sem)
                            pool.wait_ge(*o["y"](e * 2 + (2 * u0 + 2)))
                            scatter(e + b * E, 0, o["scat"].sem)
                            pool.wait_ge(*o["scat"](e * 16 + (16 * u0 + 16)))
                            step.leave(E)
                    step = main_step
                pool.sem_inc(s["scat_all"].sem, 1)
                for c in range(TC):
                    if c >= 2:
                        pool.wait_ge(*s["comb_free"](c - 1))
                    at = XN[:, (c % 2) * 2 * D:(c % 2 + 1) * 2 * D].rearrange("p (k n) -> p k n", k=2)
                    pool.dma_start(at, ys_d[l].rearrange("(k c p) n -> c p k n", k=2, p=P)[c]).then_inc(s["rows_in"][c % 2].sem, 16)
                if l == 0:
                    for c in range(TC):
                        pool.wait_ge(*s["x_new"](c + 1))
                        pool.dma_start(x1_d[c * P:(c + 1) * P, :], x3[:, c, :]).then_inc(s["x_out"].sem, 16)
                    pool.wait_ge(*s["x_out"](16 * TC))

        @block.scalar
        def _(act):
            act.dma_start(C[:, :], const).then_inc(const_in, 16)
            vecs = [(V_C, t["c"].rearrange("b (k p) -> (b k) p", p=P)),
                    (V_NA, t["norm_attn"].rearrange("l (k p) -> (l k) p", p=P)),
                    (V_NF, t["norm_ffn"].rearrange("l (k p) -> (l k) p", p=P)),
                    (V_KN, t["kv_norm"].rearrange("(k p) -> k p", p=P)),
                    (V_KAB, t["kv_ada_b"].rearrange("(k p) -> k p", p=P)),
                    (V_SUB, t["a_subln"])]
            for at, src in vecs:
                act.dma_start(W[at:at + src.shape[0], 0:P], src).then_inc(vec_in, 16)
            for at, src in ((V_QG, t["a_q_norm"]), (V_KG, t["a_k_norm"])):
                for i in range(2):
                    act.dma_start(W[at:at + 1, i * DH:(i + 1) * DH], src).then_inc(vec_in, 16)
            for at, src in ((V_BQ, t["b_q_norm"][0]), (V_BK, t["kv_k_norm"])):
                act.dma_start(W[at:at + 1, 0:P], src[0:2, :].rearrange("(o g) n -> o (g n)", o=1)).then_inc(vec_in, 16)
                for i in range(2):
                    act.dma_start(W[at + 1:at + 2, i * DH:(i + 1) * DH], src[2:3, :]).then_inc(vec_in, 16)
            act.dma_start(W[0:96, P:2 * P], t["ada_b"].rearrange("l (j p) -> (l j) p", p=P)).then_inc(vec_in, 16)
            act.dma_start(W[:, 256:512], t["a_lambda"].rearrange("o i n -> o (i n)").broadcast_to([P, 256])).then_inc(vec_in, 16)
            act.dma_start(W[:, 1792:1792 + M_END], masks[:, 0:M_END]).then_inc(vec_in, 16)
            act.dma_start(flip, masks[:, M_FLIP:M_FLIP + P]).then_inc(vec_in, 16)
            act.dma_start(V[0:BUCKETS + 1, 4096:4096 + FDIST], buckets).then_inc(bias_in, 16)
            act.dma_start(V[0:BUCKETS, 4096 + FDIST:4096 + FDIST + H], t["rel_bias"]).then_inc(bias_in, 16)
            act.dma_start(x3, t["x"][0].rearrange("(c p) n -> p c n", p=P)).then_inc(x_in, 16)
            act.wait_ge(setup_dve, 1)
            act.activation(cact[:, :], colV[:, V_C:V_C + KC], ACT.Silu).then_inc(setup_act, 1)
            act.wait_ge(setup_dve, 3)
            act.activation(lamw[:, 2:4], lamw[:, 0:2], ACT.Exp).then_inc(setup_act, 1)

            for l in range(LAYERS):
                s, o = sm[l], ov[l]

                if l == 0:
                    act.wait_ge(x_in, 16)
                else:
                    act.wait_ge(*sm[0]["x_new"](TC))
                for c in range(TC):
                    if c:
                        act.wait_ge(*s["ss_ready"](c))
                    act.activation(XN[:, 0:D], x3[:, c, :], ACT.Square,
                                   accum_out=small[:, c:c + 1]).then_inc(s["ss_ready"].sem, 1)
                act.wait_ge(*s["rms_arg"](1))
                act.activation(small[:, 8:12], small[:, 4:8], ACT.Sqrt).then_inc(s["rms_root"].sem, 1)

                u = 0
                for phase, (kind, j0, j1) in enumerate(PHASES[l]):
                    a, sh = (2, kvm[:, 0:8]) if kind == "kv" else (0, mod[:, 0:8])
                    act.wait_ge(*s["mod_ready"](phase + 1))
                    for k in range(KC):
                        act.wait_ge(*s["xt_pe"](phase * KC + k + 1))
                        if phase and k == 0:
                            act.wait_ge(*s["proj_pe"](TC * j0))
                        act.activation(ht3[:, k, :], bank[4 + k % 4][:, :], ACT.Identity,
                                       bias=sh[:, k:k + 1], scale=scl[:, a, k:k + 1]).then_inc(s["ht_ready"].sem, 1)
                    for j in range(j0, j1):
                        for c in range(TC):
                            if PROJ[l][j][0] != "v":
                                n = staged_before(l, j) + c
                                act.wait_ge(*s["proj_pe"](u + 1))
                                if n >= 2:
                                    act.wait_ge(*s["q_arg"](n - 1))
                                act.activation(W[:, HALF * (n % 2):HALF * (n % 2 + 1)], bank[u % 4][:, :],
                                               ACT.Square).then_inc(s["sq_ready"].sem, 1)
                                act.wait_ge(*s["q_arg"](n + 1))
                                act.activation(small[:, 24:32], small[:, 16:24], ACT.Sqrt).then_inc(s["q_root"].sem, 1)
                            u += 1

                if l == 0:
                    kinds = [(V_QG, 0, P), (V_KG, 1, P)]
                else:
                    kinds = [(V_BQ, 0, P), (V_BK, 1, P), (V_BQ2, 2, DH), (V_BK2, 3, DH)]
                act.wait_ge(*s["proj_free"](TC * len(PROJ[l])))
                per = 2 * len(kinds)
                with act.Fori(0, H // 2) as it:
                    for b in range(2):
                        for i, (gain, at, rows) in enumerate(kinds):
                            act.wait_ge(*s["qk_pe"](it * per + b * len(kinds) + (i + 1 + QK_CREDIT[l])))
                            if i == 0:
                                act.wait_ge(*s["s_pe"](it * 2 * TC + (CREDIT + TC * (b - 1))))
                            act.activation(X[0:rows, (4 * b + at) * S:(4 * b + at + 1) * S], bank[PART_BANK[i]][0:rows, :],
                                           ACT.Identity, scale=colV[0:rows, gain:gain + 1]).then_inc(s["qk_t"].sem, 1)
                    for v in range(2 * TC):
                        c = v % TC
                        act.wait_ge(*s["logits"](it * 2 * TC + (v + 1 + CREDIT)))
                        if l == 0:
                            n = (c + 1) * P
                            for i in range(2):
                                at = (2 * (v % 2) + i) * S
                                act.activation(W[:, at:at + n], W[:, at:at + n], ACT.Exp,
                                               bias=small[:, 2 * (v % 2) + i:2 * (v % 2) + i + 1],
                                               accum_out=small2[:, 2 * (v % 2) + i:2 * (v % 2) + i + 1]).then_inc(s["exps"].sem, 1)
                            act.wait_ge(*s["pt_pe"](it * 2 * TC + (v + 1)))
                            act.wait_ge(*s["o_pe"](it * 2 * TC + (v - 1 + CREDIT)))
                            act.activation(W[:, 2048 + S * (v % 2):2048 + S * (v % 2) + n], bank[6][:, 0:n],
                                           ACT.Identity).then_inc(s["pt"].sem, 1)
                        else:
                            n = sum(widths(l, c))
                            at = 1280 * (v % 2)
                            act.activation(W[:, at:at + n], W[:, at:at + n], ACT.Exp,
                                           bias=small[:, v % 2:v % 2 + 1],
                                           accum_out=small2[:, v % 2:v % 2 + 1]).then_inc(s["exps"].sem, 1)
                            act.wait_ge(*s["o_pe"](it * 2 * TC + (v + CREDIT)))
                            for r in range(ROUNDS[c]):
                                m = min(4 * P, n - r * 4 * P)
                                act.wait_ge(*s["pt_pe"](it * 2 * HEAD_ROUNDS + ((v // TC) * HEAD_ROUNDS + ROUND0[c] + r + 1)))
                                rr = (ROUND0[c] + r) % 2
                                act.activation(W[:, 2560 + r * 512:2560 + r * 512 + m], bank[5 + rr][:, 0:m],
                                               ACT.Identity).then_inc(s["pt"].sem, 1)

                if l == 0:
                    act.wait_ge(*s["o_out"](TC * H + CREDIT))
                    for c in range(TC):
                        if c >= 1:
                            act.wait_ge(*s["sub_arg"](c))
                        act.activation(W[:, 0:D], xn3[:, c, :], ACT.Square).then_inc(s["sub_sq"].sem, 1)
                    act.wait_ge(*s["sub_arg"](TC + 1))
                    act.activation(small2[:, 0:32], small[:, 0:32], ACT.Sqrt).then_inc(s["sub_root"].sem, 1)
                    for k in range(KC):
                        act.wait_ge(*s["ot_pe"](k + 1))
                        act.activation(ht3[:, k, :], bank[4 + k % 4][:, :], ACT.Identity,
                                       scale=colV[:, V_SUB:V_SUB + 1]).then_inc(s["ot_ready"].sem, 1)
                else:
                    for k in range(4):
                        act.wait_ge(*s["ot_pe"](k + 1))
                        act.activation(ht3[:, k, :], bank[4 + k % 4][:, :], ACT.Identity).then_inc(s["ot_ready"].sem, 1)

                for c in range(TC):
                    act.wait_ge(*s["y_added"](TC + c + 1))
                    if c:
                        act.wait_ge(*s["ss2"](c))
                    act.activation(W[:, 1024:1024 + D], x3[:, c, :], ACT.Square,
                                   accum_out=small[:, c:c + 1]).then_inc(s["ss2"].sem, 1)
                act.wait_ge(*s["arg2"](1))
                act.activation(small[:, 8:12], small[:, 4:8], ACT.Sqrt).then_inc(s["root2"].sem, 1)
                for k in range(KC):
                    act.wait_ge(*s["xt2_pe"](k + 1))
                    if k == 0:
                        act.wait_ge(*s["wo_pe"](2 * TC))
                    act.activation(ht3[:, k, :], bank[4 + k % 4][:, :], ACT.Identity,
                                   bias=mod[:, 24 + k:25 + k], scale=scl[:, 1, k:k + 1]).then_inc(s["ht2"].sem, 1)
                act.wait_ge(*s["route_e"](1))
                act.activation(small2[:, 20:36], small2[:, 20:36], ACT.Exp).then_inc(s["route_e_done"].sem, 1)
                act.wait_ge(*s["route_e"](2))
                act.activation(small2[:, 36:40], small2[:, 36:40], ACT.Exp).then_inc(s["route_e_done"].sem, 1)

                def rows_t(e, b):
                    for r in range(2):
                        act.wait_ge(*s["xr_pe"](e * 2 + (r + 1)))
                        if r == 0 and not (isinstance(e, int) and e < 2):
                            act.wait_ge(*s["gu_pe"](e * 2 - 2))
                        for q in range(4):
                            k = 4 * r + q
                            ins = act.activation(V[:, 2 * D + b * D + k * P:2 * D + b * D + (k + 1) * P],
                                                 bank[0][:, q * P:(q + 1) * P], ACT.Identity,
                                                 bias=mod[:, 24 + k:25 + k], scale=scl[:, 1, k:k + 1])
                        ins.then_inc(s["xr_t"].sem, 1)

                def silu(e, b):
                    act.wait_ge(*s["gu_pe"](e * 2 + 1))
                    act.wait_ge(*s["hid_pe"](e + (CREDIT - 1)))
                    act.activation(V[:, 4 * D + b * HALF:4 * D + (b + 1) * HALF], bank[2 + b][:, :],
                                   ACT.Silu).then_inc(s["silu"].sem, 1)

                def y_half(e, b):
                    act.wait_ge(*s["dn_pe"](e * 2 + 1))
                    act.wait_ge(*s["scat"][b]((e - b) * 8))
                    act.activation(HT[:, b * D:b * D + HALF], bank[6][:, :], ACT.Identity).then_inc(s["y_evac"].sem, 1)

                rows_t(0, 0)
                rows_t(1, 1)
                silu(0, 0)

                def expert(e, b):
                    silu(e + 1, 1 - b)
                    rows_t(e + 2, b)
                    y_half(e, b)

                for b in range(2):
                    expert(b, b)
                with act.Fori(1, 15) as it:
                    for b in range(2):
                        expert(it * 2 + b, b)
                silu(E - 1, 1)
                y_half(E - 2, 0)
                y_half(E - 1, 1)

                act.wait_ge(*s["flag_ready"](1))
                most = act.value_load(flag[0:1, 0:1], min_val=0, max_val=S)
                with act.If(most > P):
                    for bb in range(1, TC):
                        with act.Fori(0, E) as e:
                            u0 = (bb - 1) * E
                            for r in range(2):
                                act.wait_ge(*o["xr_pe"](e * 2 + (2 * u0 + r + 1)))
                                for q in range(4):
                                    k = 4 * r + q
                                    ins = act.activation(V[:, 2 * D + k * P:2 * D + (k + 1) * P],
                                                         bank[0][:, q * P:(q + 1) * P], ACT.Identity,
                                                         bias=mod[:, 24 + k:25 + k], scale=scl[:, 1, k:k + 1])
                                ins.then_inc(o["xr_t"].sem, 1)
                            act.wait_ge(*o["gu_pe"](e * 2 + (2 * u0 + 1)))
                            act.activation(V[:, 4 * D:4 * D + HALF], bank[2][:, :], ACT.Silu).then_inc(o["silu"].sem, 1)
                            act.wait_ge(*o["dn_pe"](e + (u0 + 1)))
                            act.activation(HT[:, 0:HALF], bank[6][:, :], ACT.Identity).then_inc(o["y"].sem, 1)

        @block.vector
        def _(dve):
            step = Steps(dve, dve_s)
            dve.wait_ge(setup_pe, 1)
            dve.tensor_copy(colV[:, :], bank[0][:, 0:V_END]).then_inc(setup_dve, 1)
            dve.wait_ge(setup_dve, 1)
            step(dve.tensor_scalar(colV[:, V_QG:V_QG + 1], colV[:, V_QG:V_QG + 1], DH ** -0.5, None, ALU.mult))
            step(dve.tensor_scalar(colV[:, V_BQ:V_BQ + 2], colV[:, V_BQ:V_BQ + 2], DH ** -0.5, None, ALU.mult))
            step(dve.tensor_scalar(colV[:, V_SUB:V_SUB + 1], colV[:, V_SUB:V_SUB + 1], 1 - LAM_INIT, None, ALU.mult))
            dve.wait_ge(setup_pe, 2)
            dve.tensor_copy(colA[:, :], bank[1][:, 0:96]).then_inc(setup_dve, 1)
            lp = W[:, 256:512].rearrange("p (a i n) -> p a i n", a=2, i=2)
            step(dve.tensor_tensor(W[:, 512:640].rearrange("p (a n) -> p a n", a=2),
                                   lp[:, :, 0, :], lp[:, :, 1, :], ALU.mult))
            dve.tensor_reduce(lamw[:, 0:2], W[:, 512:640].rearrange("p (a n) -> p a n", a=2), AX.X,
                              ALU.add).then_inc(setup_dve, 1)
            step(dve.tensor_copy(maskb[:, :], W[:, 1792:1792 + M_END]))
            dve.wait_ge(const_in, 16)
            step(dve.tensor_copy(identb[:, :], ident))
            step(dve.tensor_copy(aid[:, :], C[:, C_AID:C_AID + 2 * TC]))
            dve.wait_ge(setup_act, 2)
            step(dve.tensor_tensor(lamw[:, 4:5], lamw[:, 3:4], lamw[:, 2:3], ALU.subtract))
            step(dve.tensor_scalar(nlam[:, :], lamw[:, 4:5], LAM_INIT, None, ALU.subtract))
            dve.wait_ge(bias_in, 32)
            dve.memset(V[BUCKETS:BUCKETS + 1, 4096 + FDIST:4096 + FDIST + H], NEG).then_inc(setup_dve, 1)
            dve.wait_ge(setup_pe, 3)
            step(dve.tensor_copy(W[0:H, 1024:1024 + 512], bank[2][0:H, :]))
            dve.tensor_copy(W[0:H, 1536:1536 + P], bank[3][0:H, 0:P]).then_inc(setup_dve, 1)
            for h in range(H):
                dve.wait_ge(setup_pe, 4 + h)
                dve.tensor_copy(T[:, h * S:(h + 1) * S], bank[4 + h % 4][:, :]).then_inc(setup_dve, 1)

            for l in range(LAYERS):
                s, o = sm[l], ov[l]

                def norm(sq, arg, root, ready):
                    dve.wait_ge(*sq(TC))
                    dve.tensor_scalar(small[:, 4:8], small[:, 0:4], 1.0 / D, EPS, ALU.mult, ALU.add).then_inc(arg.sem, 1)
                    dve.wait_ge(*root(1))
                    step(dve.reciprocal(small[:, 12:16], small[:, 8:12]))
                    for c in range(TC):
                        dve.tensor_scalar(xn3[:, c, :], x3[:, c, :], small[:, 12 + c:13 + c], None,
                                          ALU.mult).then_inc(ready.sem, 1)

                norm(s["ss_ready"], s["rms_arg"], s["rms_root"], s["xn_ready"])

                u = 0
                for phase, (kind, j0, j1) in enumerate(PHASES[l]):
                    dve.wait_ge(*s["mod_pe"](phase + 1))
                    if kind == "kv":
                        step(dve.tensor_tensor(kvm[:, :], bank[0][:, 48:64], colV[:, V_KAB:V_KAB + 16], ALU.add))
                        dve.scalar_tensor_tensor(scl[:, 2, :], kvm[:, 8:16], 1.0, colV[:, V_KN:V_KN + KC],
                                                 ALU.add, ALU.mult).then_inc(s["mod_ready"].sem, 1)
                    else:
                        step(dve.tensor_tensor(mod[:, 0:16], bank[0][:, 0:16], colA[:, l * 48:l * 48 + 16], ALU.add))
                        dve.scalar_tensor_tensor(scl[:, 0, :], mod[:, 8:16], 1.0,
                                                 colV[:, V_NA + l * KC:V_NA + (l + 1) * KC],
                                                 ALU.add, ALU.mult).then_inc(s["mod_ready"].sem, 1)
                    for j in range(j0, j1):
                        kd, b = PROJ[l][j]
                        for c in range(TC):
                            if kd == "v":
                                dve.wait_ge(*s["proj_pe"](u + 1))
                                dve.tensor_copy(val[l][:, c, b * HALF:(b + 1) * HALF],
                                                bank[u % 4][:, :]).then_inc(s["proj_free"].sem, 1)
                            else:
                                n = staged_before(l, j) + c
                                dve.wait_ge(*s["sq_ready"](n + 1))
                                step(dve.tensor_reduce(small2[:, 0:8],
                                                       W[:, HALF * (n % 2):HALF * (n % 2 + 1)].rearrange(
                                                           "p (a n) -> p a n", n=DH), AX.X, ALU.add))
                                dve.tensor_scalar(small[:, 16:24], small2[:, 0:8], 1.0 / DH, EPS,
                                                  ALU.mult, ALU.add).then_inc(s["q_arg"].sem, 1)
                                dve.wait_ge(*s["q_root"](n + 1))
                                step(dve.reciprocal(small2[:, 8:16], small[:, 24:32]))
                                if n >= 2:
                                    dve.wait_ge(*s["stage_out"][n % 2](16 * (n // 2)))
                                at = W[:, 1024 + HALF * (n % 2):1024 + HALF * (n % 2 + 1)]
                                ins = dve.tensor_tensor(at.rearrange("p (a n) -> p a n", n=DH),
                                                        bank[u % 4][:, :].rearrange("p (a n) -> p a n", n=DH),
                                                        small2[:, 8:16].unsqueeze(2).broadcast_to([P, 8, DH]),
                                                        ALU.mult)
                                ins.then_inc(s["stage_ready"].sem, 1)
                                dve.wait_ge(*s["stage_ready"](n + 1))
                                dve.sem_inc(s["proj_free"].sem, 1)
                            u += 1
                dve.wait_ge(*s["gate_pe"](1))
                step(dve.tensor_tensor(mod[:, 16:48], bank[0][:, 16:48], colA[:, l * 48 + 16:l * 48 + 48], ALU.add))
                dve.scalar_tensor_tensor(scl[:, 1, :], mod[:, 32:40], 1.0,
                                         colV[:, V_NF + l * KC:V_NF + (l + 1) * KC],
                                         ALU.add, ALU.mult).then_inc(s["mod_ready"].sem, 1)
                dve.wait_ge(*s["gate_pe"](2))
                dve.tensor_copy(W[0:KC, 3584:3584 + 2 * P], bank[1][0:KC, 0:2 * P]).then_inc(s["gate_rows"].sem, 1)

                for i in range(2):
                    dve.wait_ge(*s["stage_out"][i](16 * (N_STAGED[l] // 2)))
                dve.wait_ge(*s["gate_out"](32))
                if l == 0:
                    dve.wait_ge(setup_dve, 13)
                dve.sem_inc(s["logits"].sem, CREDIT)
                dve.sem_inc(s["o_out"].sem, CREDIT)
                with dve.Fori(0, H // 2) as it:
                    step.enter(it, 2 * TC * (3 if l == 0 else 2))

                    def logits(v):
                        c = v % TC
                        h = it * 2 + v // TC
                        n = (c + 1) * P
                        dve.wait_ge(*s["s_pe"](it * 2 * TC + (v + 1 + CREDIT)))
                        if l == 0:
                            if v >= 2:
                                dve.wait_ge(*s["pt_pe"](it * 2 * TC + (v - 1)))
                            for i in range(2):
                                at = (2 * (v % 2) + i) * S
                                ins = dve.tensor_tensor(W[:, at:at + n], bank[2 + 2 * (v % 2) + i][:, 0:n],
                                                        T[:, ds(h * S + (S - n), n)], ALU.add)
                            step(ins)
                            at = 2 * (v % 2) * S
                            dve.tensor_reduce(small[:, 2 * (v % 2):2 * (v % 2) + 2],
                                              W[:, at:at + 2 * S].rearrange("p (i n) -> p i n", i=2)[:, :, 0:n],
                                              AX.X, ALU.max, negate=True).then_inc(s["logits"].sem, 1)
                        else:
                            if v >= 2:
                                dve.wait_ge(*s["pt_pe"](it * 2 * HEAD_ROUNDS + (
                                    ((v - 2) // TC) * HEAD_ROUNDS + ROUND0[(v - 2) % TC] + ROUNDS[(v - 2) % TC])))
                            at = 1280 * (v % 2)
                            for g, w in enumerate(widths(l, c)):
                                ins = dve.tensor_tensor(W[:, at:at + w], bank[2 + g][:, 0:w],
                                                        T[:, ds(h * S + (S - w), w)], ALU.add)
                                at += w
                            step(ins)
                            dve.tensor_reduce(small[:, v % 2:v % 2 + 1], W[:, 1280 * (v % 2):at], AX.X, ALU.max,
                                              negate=True).then_inc(s["logits"].sem, 1)

                    def probs(v):
                        c, b = v % TC, v % 2
                        n = (c + 1) * P
                        if l == 0:
                            dve.wait_ge(*s["exps"](it * 4 * TC + (2 * v + 2)))
                            step(dve.reciprocal(small2[:, 8 + 2 * b:10 + 2 * b], small2[:, 2 * b:2 * b + 2]))
                            step(dve.tensor_scalar(small2[:, 12:13], small2[:, 9 + 2 * b:10 + 2 * b],
                                                   small2[:, 2 * b:2 * b + 1], nlam[:, 0:1], ALU.mult, ALU.mult))
                            at = 2 * b * S
                            dve.scalar_tensor_tensor(W[:, at:at + n], W[:, at + S:at + S + n], small2[:, 12:13],
                                                     W[:, at:at + n], ALU.mult, ALU.add).then_inc(s["probs"].sem, 1)
                        else:
                            dve.wait_ge(*s["exps"](it * 2 * TC + (v + 1)))
                            step(dve.reciprocal(small2[:, 8 + 2 * b:9 + 2 * b], small2[:, b:b + 1]))

                    def output(v):
                        c, b = v % TC, v % 2
                        h = it * 2 + v // TC
                        w = P if l == 0 else DH
                        dve.wait_ge(*s["o_pe"](it * 2 * TC + (v + 1 + CREDIT)))
                        to = XN[:, 0:TC * H * w].rearrange("p (c n) -> p c n", c=TC)[:, c, ds(h * w, w)]
                        ins = dve.tensor_scalar(to, bank[O_BANK[v % 2]][:, 0:w], small2[:, 8 + 2 * b:9 + 2 * b],
                                                None, ALU.mult)
                        ins.then_inc(s["o_out"].sem, 1)

                    logits(0)
                    for v in range(2 * TC):
                        probs(v)
                        if v + 1 < 2 * TC:
                            logits(v + 1)
                        output(v)
                    step.leave(H // 2)

                if l == 0:
                    dve.wait_ge(*s["o_out"](CREDIT + TC * H))
                    for c in range(TC):
                        dve.wait_ge(*s["sub_sq"](c + 1))
                        dve.tensor_reduce(small2[:, c * H:(c + 1) * H],
                                          W[:, 0:D].rearrange("p (h n) -> p h n", h=H), AX.X, ALU.add).then_inc(s["sub_arg"].sem, 1)
                    dve.wait_ge(*s["sub_arg"](TC))
                    dve.tensor_scalar(small[:, 0:32], small2[:, 0:32], 1.0 / P, EPS, ALU.mult, ALU.add).then_inc(s["sub_arg"].sem, 1)
                    dve.wait_ge(*s["sub_root"](1))
                    step(dve.reciprocal(small[:, 0:32], small2[:, 0:32]))
                    for c in range(TC):
                        v3 = xn3[:, c, :].rearrange("p (h n) -> p h n", h=H)
                        dve.tensor_tensor(v3, v3, small[:, c * H:(c + 1) * H].unsqueeze(2).broadcast_to([P, H, P]),
                                          ALU.mult).then_inc(s["sub_ready"].sem, 1)

                dve.wait_ge(*s["x_re_in"](16))
                dve.wait_ge(*s["ga_in"](16))
                for u in range(2 * TC):
                    hf, c = divmod(u, TC)
                    cols = slice(hf * HALF, (hf + 1) * HALF)
                    dve.wait_ge(*s["wo_pe"](u + 1))
                    step(dve.tensor_tensor(W[:, 0:HALF], bank[u % 4][:, :], V[:, cols], ALU.mult))
                    dve.tensor_tensor(x3[:, c, cols], x3[:, c, cols], W[:, 0:HALF], ALU.add).then_inc(s["y_added"].sem, 1)
                    dve.wait_ge(*s["y_added"](u + 1))
                norm(s["ss2"], s["arg2"], s["root2"], s["xn2"])

                dve.wait_ge(*s["route_pe"](1))
                dve.wait_ge(*s["rw_in"](64))
                LG = W[:, 0:TC * NR].rearrange("p (c n) -> p c n", c=TC)
                gl, el = LG[:, :, 0:NG], LG[:, :, NG:NR]
                EQ = W[:, 144:272].rearrange("p (c n) -> p c n", c=TC)
                EQG = W[:, 144:160].rearrange("p (c n) -> p c n", c=TC)
                OH = [W[:, 272 + 128 * i:400 + 128 * i].rearrange("p (c n) -> p c n", c=TC) for i in range(2)]
                EM = W[:, 528:656].rearrange("p (c n) -> p c n", c=TC)
                M3 = W[:, 656:784].rearrange("p (c n) -> p c n", c=TC)
                RK = W[:, 784:912].rearrange("p (c n) -> p c n", c=TC)
                DF = W[:, 912:920]
                gmax, gidx, m1, i1, m2, i2 = (small2[:, 0:4], small2[:, 4:8], small2[:, 8:12], small2[:, 12:16],
                                              small2[:, 16:20], small[:, 0:4])
                eg = small2[:, 20:36].rearrange("p (c n) -> p c n", c=TC)
                e21 = small2[:, 36:40]
                gsum, gw, den, p1 = small[:, 4:8], small[:, 8:12], small[:, 12:16], small[:, 16:20]
                pen = small[:, 20:36]
                pen3 = pen.rearrange("p (c n) -> p c n", c=TC)

                def over(a, n):
                    return a.unsqueeze(2).broadcast_to([P, TC, n])

                def per_chunk(a, n):
                    return a.unsqueeze(1).broadcast_to([P, TC, n])

                step(dve.tensor_tensor(LG, bank[0][:, 0:TC * NR].rearrange("p (c n) -> p c n", c=TC),
                                       per_chunk(rbias[:, :], NR), ALU.add))
                iog, ioe = per_chunk(C[:, C_IG:C_IG + NG], NG), per_chunk(C[:, C_IE:C_IE + E], E)
                step(dve.tensor_reduce(gmax, gl, AX.X, ALU.max))
                step(dve.tensor_tensor(EQG, gl, over(gmax, NG), ALU.is_equal))
                step(dve.tensor_tensor(EQG, EQG, iog, ALU.mult))
                step(dve.tensor_reduce(gidx, EQG, AX.X, ALU.min))
                step(dve.tensor_tensor(pen3, iog, over(gidx, NG), ALU.is_equal))
                dve.tensor_tensor(eg, gl, over(gmax, NG), ALU.subtract).then_inc(s["route_e"].sem, 1)
                step(dve.tensor_scalar(pen, pen, -NEG, NEG, ALU.mult, ALU.add))
                step(dve.tensor_tensor(EM.rearrange("p c (g n) -> p c g n", g=NG),
                                       el.rearrange("p c (g n) -> p c g n", g=NG),
                                       pen3.unsqueeze(3).broadcast_to([P, TC, NG, PER_G]), ALU.add))
                for i, (m, ix) in enumerate(((m1, i1), (m2, i2))):
                    step(dve.tensor_reduce(m, EM, AX.X, ALU.max))
                    step(dve.tensor_tensor(EQ, EM, over(m, E), ALU.is_equal))
                    step(dve.tensor_tensor(EQ, EQ, ioe, ALU.mult))
                    step(dve.tensor_reduce(ix, EQ, AX.X, ALU.min))
                    step(dve.tensor_tensor(OH[i], ioe, over(ix, E), ALU.is_equal))
                    if i == 0:
                        step(dve.scalar_tensor_tensor(EM, OH[0], 2 * NEG, EM, ALU.mult, ALU.add))
                dve.tensor_tensor(M3, OH[0], OH[1], ALU.add).then_inc(s["picked"].sem, 1)
                dve.tensor_tensor(e21, m2, m1, ALU.subtract).then_inc(s["route_e"].sem, 1)
                dve.wait_ge(*s["route_e_done"](1))
                step(dve.tensor_reduce(gsum, eg, AX.X, ALU.add))
                step(dve.reciprocal(gw, gsum))
                dve.wait_ge(*s["route_e_done"](2))
                step(dve.tensor_scalar(den, e21, 1.0, None, ALU.add))
                step(dve.reciprocal(p1, den))
                step(dve.tensor_tensor(gates[:, 0, :], p1, gw, ALU.mult))
                step(dve.tensor_tensor(gates[:, 1, :], gates[:, 0, :], e21, ALU.mult))
                dve.wait_ge(*s["rank_pe"](1))
                step(dve.tensor_tensor(RK, bank[1][:, 0:TC * E].rearrange("p (c n) -> p c n", c=TC),
                                       per_chunk(C[:, C_E512:C_E512 + E], E), ALU.add))
                step(dve.tensor_reduce(DF[:, 0:1], bank[1][:, TC * E:TC * E + E], AX.X, ALU.max))
                dve.tensor_copy(flag[:, :], DF[:, 0:1]).then_inc(s["flag_ready"].sem, 1)
                dve.wait_ge(*s["flag_ready"](1))
                for i in range(2):
                    step(dve.tensor_tensor(EQ, OH[i], RK, ALU.mult))
                    step(dve.tensor_reduce(DF[:, 4 * i:4 * i + 4], EQ, AX.X, ALU.add))
                dve.tensor_copy(dest[:, :], DF).then_inc(s["dest_ready"].sem, 1)
                dve.wait_ge(*s["tab_back"](16))
                dve.tensor_copy(W[0:E, 2560:2560 + S], W[0:E, 3072:3072 + S].bitcast(I32)).then_inc(s["tab_f"].sem, 1)
                dve.wait_ge(*s["tab_pe"](1))
                step(dve.tensor_copy(dst[:, :], bank[2][:, 0:P]))
                step(dve.tensor_scalar(W[:, 1024:1024 + P], bank[2][:, 0:P], float(S), float(-S), ALU.is_ge, ALU.mult))
                dve.tensor_tensor(tok[:, :], bank[2][:, 0:P], W[:, 1024:1024 + P], ALU.add).then_inc(s["tok_ready"].sem, 1)

                def hidden(e, b):
                    dve.wait_ge(*s["silu"](e + 1))
                    dve.wait_ge(*s["gu_pe"](e * 2 + 2))
                    at = V[:, 4 * D + b * HALF:4 * D + (b + 1) * HALF]
                    dve.tensor_tensor(at, at, bank[4 + b][:, :], ALU.mult).then_inc(s["hid"].sem, 1)

                def hidden_t(e, b):
                    dve.wait_ge(*s["hid_pe"](e + (1 + CREDIT)))
                    if not (isinstance(e, int) and e < 2):
                        dve.wait_ge(*s["dn_pe"](e * 2 - 2))
                    dve.tensor_copy(V[:, 5 * D + b * HALF:5 * D + (b + 1) * HALF], bank[1][:, :]).then_inc(s["hid_t"].sem, 1)

                def y_half(e, b):
                    dve.wait_ge(*s["dn_pe"](e * 2 + 2))
                    dve.wait_ge(*s["y_evac"](e * 2 + 1))
                    dve.wait_ge(*s["scat"][b]((e - b) * 8))
                    dve.tensor_copy(HT[:, b * D + HALF:(b + 1) * D], bank[7][:, :]).then_inc(s["y_evac"].sem, 1)

                hidden(0, 0)
                hidden_t(0, 0)
                hidden(1, 1)
                y_half(0, 0)
                hidden_t(1, 1)
                hidden(2, 0)
                y_half(1, 1)
                with dve.Fori(1, 15) as it:
                    for b in range(2):
                        e = it * 2 + b
                        hidden_t(e, b)
                        hidden(e + 1, 1 - b)
                        y_half(e, b)
                hidden_t(E - 2, 0)
                hidden(E - 1, 1)
                y_half(E - 2, 0)
                hidden_t(E - 1, 1)
                y_half(E - 1, 1)

                most = dve.value_load(flag[0:1, 0:1], min_val=0, max_val=S)
                with dve.If(most > P):
                    for bb in range(1, TC):
                        with dve.Fori(0, E) as e:
                            u0 = (bb - 1) * E
                            dve.wait_ge(*o["silu"](e + (u0 + 1)))
                            dve.wait_ge(*o["gu_pe"](e * 2 + (2 * u0 + 2)))
                            at = V[:, 4 * D:4 * D + HALF]
                            dve.tensor_tensor(at, at, bank[4][:, :], ALU.mult).then_inc(o["hid"].sem, 1)
                            dve.wait_ge(*o["hid_pe"](e + (u0 + 1)))
                            dve.tensor_copy(V[:, 5 * D:5 * D + HALF], bank[1][:, :]).then_inc(o["hid_t"].sem, 1)
                            dve.wait_ge(*o["y"](e * 2 + (2 * u0 + 1)))
                            dve.tensor_copy(HT[:, HALF:D], bank[7][:, :]).then_inc(o["y"].sem, 1)

                dve.wait_ge(*s["gf_in"](16))
                for c in range(TC):
                    dve.wait_ge(*s["rows_in"][c % 2](16 * (c // 2 + 1)))
                    r0 = XN[:, (c % 2) * 2 * D:(c % 2) * 2 * D + D]
                    r1 = XN[:, (c % 2) * 2 * D + D:(c % 2 + 1) * 2 * D]
                    step(dve.tensor_scalar(r0, r0, gates[:, 0, c:c + 1], None, ALU.mult))
                    step(dve.scalar_tensor_tensor(r0, r1, gates[:, 1, c:c + 1], r0, ALU.mult, ALU.add))
                    step(dve.tensor_tensor(r0, r0, W[:, 0:D], ALU.mult))
                    dve.tensor_tensor(x3[:, c, :], x3[:, c, :], r0, ALU.add).then_inc(s["x_new"].sem, 1)
                    dve.wait_ge(*s["x_new"](c + 1))
                    dve.sem_inc(s["comb_free"].sem, 1)

        @block.tensor
        def _(pe):
            pe.wait_ge(const_in, 16)
            pe.wait_ge(vec_in, 16 * N_VEC)
            pe.transpose(bank[0][:, 0:V_END], W[0:V_END, 0:P], ident[0:V_END, 0:V_END]).then_inc(setup_pe, 1)
            pe.transpose(bank[1][:, 0:96], W[0:96, P:2 * P], ident[0:96, 0:96]).then_inc(setup_pe, 1)
            pe.wait_ge(setup_dve, 4)
            rel = V[0:BUCKETS + 1, 4096 + FDIST:4096 + FDIST + H]
            pe.matmul(bank[2][0:H, :], rel, V[0:BUCKETS + 1, 4096:4096 + 512], start=True, stop=True)
            pe.matmul(bank[3][0:H, 0:P], rel, V[0:BUCKETS + 1, 4608:4608 + P], start=True, stop=True).then_inc(setup_pe, 1)
            pe.wait_ge(setup_act, 1)

            def mod_columns(n0, nb, col0):
                for i in range(nb):
                    arrived(pe, n0 + i)
                    for m in range(4):
                        j = col0 + 4 * i + m
                        for k in range(KC):
                            ins = pe.matmul(bank[0][:, j:j + 1], slot3(n0 + i)[:, k, m * P:(m + 1) * P],
                                            cact[:, k:k + 1], start=(k == 0), stop=(k == KC - 1))
                    ins.then_inc(w_used, 1)
                return ins

            for l in range(LAYERS):
                s, o = sm[l], ov[l]
                u = 0
                for phase, (kind, j0, j1) in enumerate(PHASES[l]):
                    if kind == "kv":
                        mod_columns(START[l, "kvmod"], 4, 48)
                    else:
                        mod_columns(START[l, "mod"], 4, 0)
                    pe.wait_ge(w_used, START[l, "kvmod" if kind == "kv" else "mod"] + 4)
                    pe.sem_inc(s["mod_pe"].sem, 1)
                    if phase == 0:
                        if l == 0:
                            pe.wait_ge(hank_in, 16)
                            for h in range(H):
                                if h >= 4:
                                    pe.wait_ge(setup_dve, 2 + h)
                                pe.matmul(bank[4 + h % 4][:, :], flip, V[:, h * S:(h + 1) * S], start=True,
                                          stop=True).then_inc(setup_pe, 1)
                            pe.wait_ge(setup_dve, 13)
                        pe.wait_ge(*s["xn_ready"](TC))
                    for k in range(KC):
                        if phase * KC + k >= 4:
                            pe.wait_ge(*s["ht_ready"](phase * KC + k - 3))
                        for c in range(TC):
                            ins = pe.transpose(bank[4 + k % 4][:, c * P:(c + 1) * P], xn3[:, c, k * P:(k + 1) * P], ident)
                        ins.then_inc(s["xt_pe"].sem, 1)
                    if phase == 0:
                        pe.wait_ge(*s["mod_ready"](1))
                    for j in range(j0, j1):
                        n = START[l, kind] + j - j0
                        arrived(pe, n)
                        for c in range(TC):
                            if u >= 4:
                                pe.wait_ge(*s["proj_free"](u - 3))
                            if phase and j == j0 and c == 0:
                                pe.wait_ge(*s["mod_ready"](phase + 1))
                            for k in range(KC):
                                if j == j0 and c == 0:
                                    pe.wait_ge(*s["ht_ready"](phase * KC + k + 1))
                                ins = pe.matmul(bank[u % 4][:, :], ht3[:, k, c * P:(c + 1) * P], slot3(n)[:, k, :],
                                                start=(k == 0), stop=(k == KC - 1))
                            ins.then_inc(s["proj_pe"].sem, 1)
                            u += 1
                        pe.wait_ge(*s["proj_pe"](u))
                        pe.sem_inc(w_used, 1)
                    pe.wait_ge(*s["proj_free"](u))
                mod_columns(START[l, "gates"], 8, 16)
                pe.wait_ge(w_used, START[l, "gates"] + 8)
                pe.sem_inc(s["gate_pe"].sem, 1)
                pe.wait_ge(*s["mod_ready"](len(PHASES[l]) + 1))
                pe.transpose(bank[1][0:KC, 0:P], mod[:, 16:24], ident)
                pe.transpose(bank[1][0:KC, P:2 * P], mod[:, 40:48], ident).then_inc(s["gate_pe"].sem, 1)
                pe.wait_ge(*s["gate_rows"](1))

                pe.sem_inc(s["qk_pe"].sem, QK_CREDIT[l])
                pe.sem_inc(s["s_pe"].sem, CREDIT)
                pe.sem_inc(s["o_pe"].sem, CREDIT)
                hw = P if l == 0 else GROUPS * DH
                parts = [(0, 0, P), (1, 0, P)] if l == 0 else [(0, 0, P), (1, 0, P), (0, P, DH), (1, P, DH)]
                nparts = len(parts)
                with pe.Fori(0, H // 2) as it:
                    for b in range(2):
                        pe.wait_ge(*s["stage_in"][b](it * STAGE_DMAS[l] + STAGE_DMAS[l]))
                        pe.wait_ge(*s["qk_t"](it * 2 * nparts + b * nparts))
                        if b == 0:
                            pe.wait_ge(*s["o_out"](it * 2 * TC + CREDIT))
                        for i, (qk, c0, w) in enumerate(parts):
                            src = HT[:, (2 * b + qk) * 768:(2 * b + qk) * 768 + TC * hw].rearrange(
                                "p (c n) -> p c n", c=TC)
                            for c in range(TC):
                                ins = pe.transpose(bank[PART_BANK[i]][0:w, c * P:(c + 1) * P], src[:, c, c0:c0 + w], ident)
                            ins.then_inc(s["qk_pe"].sem, 1)

                    def scores(v):
                        hb, c = divmod(v, TC)
                        pe.wait_ge(*s["qk_t"](it * 2 * nparts + nparts * (hb + 1)))
                        n = (c + 1) * P
                        q = [X[:, (4 * hb + i) * S + c * P:(4 * hb + i) * S + (c + 1) * P] for i in (0, 2)]
                        k = [X[:, (4 * hb + i) * S:(4 * hb + i + 1) * S] for i in (1, 3)]
                        if l == 0:
                            pe.wait_ge(*s["logits"](it * 2 * TC + (v - 1 + CREDIT)))
                            for i in range(2):
                                r = slice(i * DH, (i + 1) * DH)
                                ins = pe.matmul(bank[2 + 2 * (v % 2) + i][:, 0:n], q[0][r], k[0][r, 0:n],
                                                start=True, stop=True)
                        else:
                            pe.wait_ge(*s["logits"](it * 2 * TC + (v + CREDIT)))
                            w0 = widths(l, c)[0]
                            for g, (qq, kk, r, k0, w, m0, m1) in enumerate((
                                    (q[0], k[0], slice(0, DH), n - w0, w0, 2 * P - w0, 2 * P),
                                    (q[0], k[0], slice(DH, P), 0, n, M_4 + S - n, M_4 + S),
                                    (q[1], k[1], slice(0, DH), 0, n, M_16 + S - n, M_16 + S))):
                                pe.matmul(bank[2 + g][:, 0:w], qq[r], kk[r, k0:k0 + w], start=True, stop=False)
                                ins = pe.matmul(bank[2 + g][:, 0:w], identb[:, :], maskb[:, m0:m1],
                                                start=False, stop=True)
                        ins.then_inc(s["s_pe"].sem, 1)

                    def values(v):
                        hb, c = divmod(v, TC)
                        h = it * 2 + hb
                        if l == 0:
                            pe.wait_ge(*s["probs"](it * 2 * TC + (v + 1)))
                            pe.wait_ge(*s["pt"](it * 2 * TC + v))
                            for i in range(c + 1):
                                at = 2 * (v % 2) * S + i * P
                                ins = pe.transpose(bank[6][:, i * P:(i + 1) * P], W[:, at:at + P], ident)
                            ins.then_inc(s["pt_pe"].sem, 1)
                            pe.wait_ge(*s["pt"](it * 2 * TC + (v + 1)))
                            pe.wait_ge(*s["o_out"](it * 2 * TC + (v - 1 + CREDIT)))
                            for i in range(c + 1):
                                at = 2048 + S * (v % 2) + i * P
                                ins = pe.matmul(bank[O_BANK[v % 2]][:, 0:P], W[:, at:at + P],
                                                val[0][:, i, ds(h * P, P)], start=(i == 0), stop=(i == c))
                            ins.then_inc(s["o_pe"].sem, 1)
                        else:
                            pe.wait_ge(*s["exps"](it * 2 * TC + (v + 1)))
                            w0 = widths(l, c)[0] // P
                            keys = [(0, c + 1 - w0 + i) for i in range(w0)] + [(g, i) for g in (1, 2) for i in range(c + 1)]
                            for r in range(ROUNDS[c]):
                                done = hb * HEAD_ROUNDS + ROUND0[c] + r
                                pe.wait_ge(*s["pt"](it * 2 * HEAD_ROUNDS + max(done - 1, 0)))
                                rr = (ROUND0[c] + r) % 2
                                for i in range(4 * r, min(4 * r + 4, len(keys))):
                                    at = 1280 * (v % 2) + i * P
                                    ins = pe.transpose(bank[5 + rr][:, (i % 4) * P:(i % 4 + 1) * P], W[:, at:at + P], ident)
                                ins.then_inc(s["pt_pe"].sem, 1)
                            pe.wait_ge(*s["pt"](it * 2 * HEAD_ROUNDS + (hb * HEAD_ROUNDS + ROUND0[c] + ROUNDS[c])))
                            pe.wait_ge(*s["o_out"](it * 2 * TC + (v - 1 + CREDIT)))
                            for i, (g, kc) in enumerate(keys):
                                ins = pe.matmul(bank[O_BANK[v % 2]][:, 0:DH], W[:, 2560 + i * P:2560 + (i + 1) * P],
                                                val[1][:, kc, ds(h * DH + g * HALF, DH)],
                                                start=(i == 0), stop=(i == len(keys) - 1))
                            ins.then_inc(s["o_pe"].sem, 1)

                    scores(0)
                    for v in range(2 * TC):
                        if v + 1 < 2 * TC:
                            scores(v + 1)
                        values(v)

                ok = KC if l == 0 else 4
                ow = D if l == 0 else HALF
                o3 = XN[:, 0:TC * ow].rearrange("p (c n) -> p c n", c=TC)
                if l == 0:
                    pe.wait_ge(*s["sub_ready"](TC))
                else:
                    pe.wait_ge(*s["o_out"](CREDIT + TC * H))
                for k in range(ok):
                    if k >= 4:
                        pe.wait_ge(*s["ot_ready"](k - 3))
                    for c in range(TC):
                        ins = pe.transpose(bank[4 + k % 4][:, c * P:(c + 1) * P], o3[:, c, k * P:(k + 1) * P], ident)
                    ins.then_inc(s["ot_pe"].sem, 1)
                pe.wait_ge(*s["ot_ready"](ok))
                for u in range(2 * TC):
                    hf, c = divmod(u, TC)
                    n = START[l, "wo"] + (hf if l == 0 else 0)
                    arrived(pe, n)
                    if u >= 4:
                        pe.wait_ge(*s["y_added"](u - 3))
                    w3 = slot3(n, ok)
                    for k in range(ok):
                        rhs = w3[:, k, :] if l == 0 else w3[:, k, hf * HALF:(hf + 1) * HALF]
                        ins = pe.matmul(bank[u % 4][:, :], ht3[:, k, c * P:(c + 1) * P], rhs,
                                        start=(k == 0), stop=(k == ok - 1))
                    ins.then_inc(s["wo_pe"].sem, 1)
                    if c == TC - 1 and (l == 0 or hf == 1):
                        pe.wait_ge(*s["wo_pe"](u + 1))
                        pe.sem_inc(w_used, 1)
                pe.wait_ge(*s["xn2"](TC))
                for k in range(KC):
                    if k >= 4:
                        pe.wait_ge(*s["ht2"](k - 3))
                    for c in range(TC):
                        ins = pe.transpose(bank[4 + k % 4][:, c * P:(c + 1) * P], xn3[:, c, k * P:(k + 1) * P], ident)
                    ins.then_inc(s["xt2_pe"].sem, 1)
                pe.wait_ge(*s["ht2"](KC))
                pe.wait_ge(*s["rw_in"](64))
                pe.wait_ge(*s["y_added"](2 * TC))
                for c in range(TC):
                    for k in range(KC):
                        ins = pe.matmul(bank[0][:, c * NR:(c + 1) * NR], ht3[:, k, c * P:(c + 1) * P],
                                        rw3[:, k, :], start=(k == 0), stop=(k == KC - 1))
                ins.then_inc(s["route_pe"].sem, 1)
                pe.wait_ge(*s["picked"](1))
                m3 = W[:, 656:784].rearrange("p (c n) -> p c n", c=TC)
                for c in range(TC):
                    for cc in range(c + 1):
                        pe.matmul(bank[1][:, c * E:(c + 1) * E], tri if cc == c else ones, m3[:, cc, :],
                                  start=(cc == 0), stop=(cc == c))
                for cc in range(TC):
                    ins = pe.matmul(bank[1][:, TC * E:TC * E + E], ones, m3[:, cc, :],
                                    start=(cc == 0), stop=(cc == TC - 1))
                ins.then_inc(s["rank_pe"].sem, 1)
                pe.wait_ge(*s["tab_f"](1))
                for b in range(TC):
                    ins = pe.transpose(bank[2][:, b * E:(b + 1) * E], W[0:E, 2560 + b * P:2560 + (b + 1) * P],
                                       ident[0:E, 0:E])
                ins.then_inc(s["tab_pe"].sem, 1)
                pe.wait_ge(*s["tok_ready"](1))

                m = START[l, "moe"]
                pe.sem_inc(s["hid_pe"].sem, CREDIT)

                def rows(e, b, r):
                    if r == 0:
                        pe.wait_ge(*s["gath"][b]((e - b) * 8 + 16))
                    if not (isinstance(e, int) and e == 0 and r == 0):
                        pe.wait_ge(*s["xr_t"](e * 2 + r))
                    for q in range(4):
                        k = 4 * r + q
                        ins = pe.transpose(bank[0][:, q * P:(q + 1) * P], V[:, b * D + k * P:b * D + (k + 1) * P], ident)
                    ins.then_inc(s["xr_pe"].sem, 1)

                def gate_up(e, b, n, turn):
                    pe.wait_ge(*s["xr_t"](e * 2 + 2))
                    if not (isinstance(e, int) and e < 2):
                        pe.wait_ge(*s["hid"](e - 1))
                    for i in range(2):
                        arrived(pe, n + i, turn)
                        for k in range(KC):
                            at = 2 * D + b * D + k * P
                            ins = pe.matmul(bank[2 + 2 * i + b][:, :], V[:, at:at + P], slot3(n + i)[:, k, :],
                                            start=(k == 0), stop=(k == KC - 1))
                        ins.then_inc(s["gu_pe"].sem, 1)
                        pe.wait_ge(*s["gu_pe"](e * 2 + (i + 1)))
                        pe.sem_inc(w_used, 1)

                def down(e, b, n, turn, more):
                    pe.wait_ge(*s["hid"](e + 1))
                    if not (isinstance(e, int) and e == 0):
                        pe.wait_ge(*s["hid_t"](e))
                    for k in range(4):
                        at = 4 * D + b * HALF + k * P
                        ins = pe.transpose(bank[1][:, k * P:(k + 1) * P], V[:, at:at + P], ident)
                    ins.then_inc(s["hid_pe"].sem, 1)
                    if more:
                        rows(e + 2, b, 0)
                    arrived(pe, n, turn)
                    pe.wait_ge(*s["hid_t"](e + 1))
                    if not (isinstance(e, int) and e == 0):
                        pe.wait_ge(*s["y_evac"](e * 2))
                    for hf in range(2):
                        if hf and more:
                            rows(e + 2, b, 1)
                        for k in range(4):
                            at = 5 * D + b * HALF + k * P
                            ins = pe.matmul(bank[6 + hf][:, :], V[:, at:at + P],
                                            slot3(n, 4)[:, k, hf * HALF:(hf + 1) * HALF],
                                            start=(k == 0), stop=(k == 3))
                        ins.then_inc(s["dn_pe"].sem, 1)
                    pe.wait_ge(*s["dn_pe"](e * 2 + 2))
                    pe.sem_inc(w_used, 1)

                for b in range(2):
                    for r in range(2):
                        rows(b, b, r)
                gate_up(0, 0, m, 0)
                with pe.Fori(0, 15) as it:
                    for b in range(2):
                        e = it * 2 + b
                        gate_up(e + 1, 1 - b, m + 2 + 3 * b, it)
                        down(e, b, m + 4 + 3 * b, it, True)
                gate_up(E - 1, 1, m + 92, 0)
                down(E - 2, 0, m + 94, 0, False)
                down(E - 1, 1, m + 95, 0, False)

                most = pe.value_load(flag[0:1, 0:1], min_val=0, max_val=S)
                with pe.If(most > P):
                    pe.wait_ge(*s["y_evac"](2 * E))
                    for bb in range(1, TC):
                        with pe.Fori(0, E) as e:
                            u0 = (bb - 1) * E
                            pe.wait_ge(*o["g"](e * 16 + (16 * u0 + 16)))
                            for r in range(2):
                                pe.wait_ge(*o["xr_t"](e * 2 + (2 * u0 + r)))
                                for q in range(4):
                                    k = 4 * r + q
                                    ins = pe.transpose(bank[0][:, q * P:(q + 1) * P], V[:, k * P:(k + 1) * P], ident)
                                ins.then_inc(o["xr_pe"].sem, 1)
                            pe.wait_ge(*o["xr_t"](e * 2 + (2 * u0 + 2)))
                            pe.wait_ge(*o["w"](e * 48 + (48 * u0 + 48)))
                            for i in range(2):
                                for k in range(KC):
                                    ins = pe.matmul(bank[2 + 2 * i][:, :], V[:, 2 * D + k * P:2 * D + (k + 1) * P],
                                                    slot3(i)[:, k, :], start=(k == 0), stop=(k == KC - 1))
                                ins.then_inc(o["gu_pe"].sem, 1)
                            pe.wait_ge(*o["hid"](e + (u0 + 1)))
                            for k in range(4):
                                ins = pe.transpose(bank[1][:, k * P:(k + 1) * P],
                                                   V[:, 4 * D + k * P:4 * D + (k + 1) * P], ident)
                            ins.then_inc(o["hid_pe"].sem, 1)
                            pe.wait_ge(*o["hid_t"](e + (u0 + 1)))
                            for hf in range(2):
                                for k in range(4):
                                    ins = pe.matmul(bank[6 + hf][:, :], V[:, 5 * D + k * P:5 * D + (k + 1) * P],
                                                    slot3(2, 4)[:, k, hf * HALF:(hf + 1) * HALF],
                                                    start=(k == 0), stop=(k == 3))
                            ins.then_inc(o["dn_pe"].sem, 1)
                    pe.wait_ge(*o["y"](2 * (TC - 1) * E))


N_VEC = 6 + 4 + 6 + 4
O_BANK = (7, 1)
PART_BANK = (0, 1, 5, 6)
QK_STEPS = (2, 4)
QK_CREDIT = (4, 8)
STAGE_DMAS = (2 * 16, 8 * 16)
ROUNDS = (1, 2, 2, 3)
ROUND0 = (0, 1, 3, 5)
HEAD_ROUNDS = 8


_INS = ['x', 'c', 'rel_bias', 'ada_w', 'ada_b', 'norm_attn', 'norm_ffn', 'a_w_qkv', 'a_q_norm', 'a_k_norm',
        'a_lambda', 'a_subln', 'a_w_o', 'kv_norm', 'kv_ada_w', 'kv_ada_b', 'kv_w', 'kv_k_norm',
        'b_w_q', 'b_q_norm', 'b_w_o', 'moe_w_group', 'moe_b_group', 'moe_w_expert', 'moe_b_expert',
        'moe_w_gate', 'moe_w_up', 'moe_w_down']


def kernel(**inputs):
    import concourse.bacc as _bacc
    from concourse.bass_utils import run_bass_kernel_spmd as _run

    nc = _bacc.Bacc("TRN2", target_bir_lowering=False, num_devices=1)
    arrays, t = {}, {}

    def declare(name, a):
        arrays[f"in_{name}_dram"] = a
        return nc.dram_tensor(f"in_{name}_dram", a.shape, mybir.dt.from_np(a.dtype), kind="ExternalInput").ap()

    for name in _INS:
        t[name] = declare(name, np.ascontiguousarray(inputs[name]))
    c, m = constants()
    const, masks, buckets = declare("const", c), declare("masks", m), declare("buckets", bucket_table())
    out = nc.dram_tensor("out_0_dram", (1, S, D), F32, kind="ExternalOutput").ap()
    program(nc, t, const, masks, buckets, out)
    r = _run(nc, [arrays], core_ids=[0])
    return r.results[0]["out_0_dram"]
```

```python
import math
from contextlib import ExitStack

import numpy as np

import concourse.bass as bass
from concourse import mybir

F32 = mybir.dt.float32
BF16 = mybir.dt.bfloat16
I32 = mybir.dt.int32
ALU = mybir.AluOpType
ACT = mybir.ActivationFunctionType
AX = mybir.AxisListType
ds = bass.ds

P = 128
D = 1024
S = 512
LAYERS = 2
KC = D // P
TC = S // P
H = 8
DH = 64
GROUPS = 3
BUCKETS, MAX_EXACT, MAX_DIST = 32, 16, 2048
NG, PER_G, E, HID = 4, 8, 32, 512
NR = NG + E
EPS = 1e-6
LAM_INIT = 0.8 - 0.6 * math.exp(-0.3 * 0)
NEG = -1e30
RING = 6
HALF = 512
UNUSED = 4096
CREDIT = 4
FDIST = S + P

C_ID, C_TRI, C_ONE = 0, 128, 256
C_E512, C_IE, C_IG, C_AID = 384, 416, 448, 452
C_END = 460
M_BAND, M_4, M_16, M_END = 0, 256, 768, 1280
M_FLIP = M_END

V_C, V_NA, V_NF, V_KN, V_KAB = 0, 8, 24, 40, 48
V_QG, V_KG, V_SUB, V_BQ, V_BQ2, V_BK, V_BK2 = 64, 65, 66, 67, 68, 69, 70
V_END = 71

N_MOD = 12 + 4 + 12
MOE_BLOCKS = 3 * E


def block_order():
    order = [("mod", 0, i) for i in range(4)]
    mods = [("mod", 0, i) for i in range(4, N_MOD)]
    for kind, n in (("proj", 6), ("wo", 2)):
        for j in range(n):
            order += [(kind, 0, j)] + mods[:3]
            mods = mods[3:]
    order += [("moe", 0, i) for i in range(MOE_BLOCKS)]
    order += [("proj", 1, j) for j in range(9)] + [("wo", 1, 0)]
    order += [("moe", 1, i) for i in range(MOE_BLOCKS)]
    return order


ORDER = block_order()
AT = {b: n for n, b in enumerate(ORDER)}


def parts_after(l, v):
    return ([[0], [1], [], []] if l == 0 else [[0, 1], [2, 3], [], []])[v % TC]


def mods_after(phase, shift=0):
    first, n = (4, 6) if phase == "proj" else (22, 2)
    return {4 * j + i + shift: first + 3 * j + i for j in range(n) for i in range(3)}


def bucket_table():
    dist = (S - 1) - np.arange(FDIST)
    n = np.maximum(dist, 0)
    nf = np.maximum(n, 1).astype(np.float32)
    large = MAX_EXACT + (np.log(nf / MAX_EXACT) / math.log(MAX_DIST / MAX_EXACT)
                         * (BUCKETS - MAX_EXACT)).astype(np.int32)
    bucket = np.where(n < MAX_EXACT, n, np.minimum(large, BUCKETS - 1))
    out = np.zeros((BUCKETS + 1, FDIST), np.float32)
    out[bucket, np.arange(FDIST)] = (dist >= 0)
    out[BUCKETS] = (dist < 0)
    return out


def constants():
    p = np.arange(P)[:, None]
    c = np.zeros((P, C_END), np.float32)
    c[:, C_ID:C_ID + P] = np.eye(P)
    c[:, C_TRI:C_TRI + P] = p < np.arange(P)[None, :]
    c[:, C_ONE:C_ONE + P] = 1.0
    c[:, C_E512:C_E512 + E] = S * np.arange(E)
    c[:, C_IE:C_IE + E] = np.arange(E) - 64
    c[:, C_IG:C_IG + NG] = np.arange(NG) - 64
    c[:, C_AID:C_AID + 2 * TC] = p + P * np.arange(2 * TC)
    m = np.zeros((P, M_END + P), np.float32)
    m[:, M_FLIP:M_FLIP + P] = np.eye(P)[::-1]
    m[:, M_BAND:M_4][p + P - np.arange(2 * P)[None, :] > P] = NEG
    for at, dil in ((M_4, 4), (M_16, 16)):
        m[:, at:at + S][(p + 3 * P - np.arange(S)[None, :]) % dil != 0] = NEG
    return c, m


class Steps:

    def __init__(self, eng, sem):
        self.eng, self.sem, self.base, self.n, self.it, self.per = eng, sem, 0, 0, 0, 0

    def __call__(self, ins):
        ins.then_inc(self.sem, 1)
        self.n += 1
        self.eng.wait_ge(self.sem, self.it * self.per + (self.base + self.n))

    def enter(self, it, per):
        self.base, self.n, self.it, self.per = self.base + self.n, 0, it, per

    def leave(self, times):
        assert self.n == self.per, (self.n, self.per)
        self.base, self.n, self.it, self.per = self.base + self.per * times, 0, 0, 0


class Signal:

    def __init__(self, sem, base):
        self.sem, self.base = sem, base

    def __call__(self, value):
        return self.sem, value + self.base


def program(nc, t, const, masks, buckets, out):
    with ExitStack() as ctx:
        def sb(name, shape, dt=F32):
            return ctx.enter_context(nc.sbuf_tensor(name, shape, dt))

        def sem(name):
            return ctx.enter_context(nc.semaphore(name))

        def dram(name, shape, dt=F32):
            return nc.dram_tensor(name, shape, dt, kind="Internal").ap()

        ring = sb("ring", [P, RING, KC * HALF])
        X = sb("X", [P, TC * D])
        XN = sb("XN", [P, TC * D])
        HT = sb("HT", [P, KC * S])
        T = sb("T", [P, H * S])
        V = sb("V", [P, TC * GROUPS * HALF])
        W = sb("W", [P, 3840])
        C = sb("C", [P, C_END])
        maskb = sb("maskb", [P, M_END], BF16)
        identb = sb("identb", [P, P], BF16)
        colA = sb("colA", [P, LAYERS * 48])
        colV = sb("colV", [P, V_END])
        cact = sb("cact", [P, KC])
        mod = sb("mod", [P, 48])
        kvm = sb("kvm", [P, 16])
        scl = sb("scl", [P, 3, KC])
        lamw = sb("lamw", [P, 8])
        nlam = sb("nlam", [P, 1])
        rw = sb("rw", [P, KC * NR])
        rbias = sb("rbias", [P, NR])
        small = sb("small", [P, 48])
        small2 = sb("small2", [P, 40])
        gates = sb("gates", [P, 2, TC])
        dest = sb("dest", [P, 2 * TC], I32)
        aid = sb("aid", [P, 2 * TC], I32)
        tokc, dstc = sb("tokc", [P, 2], I32), sb("dstc", [P, 2], I32)
        pause = sb("pause", [P, 1])
        flag = sb("flag", [P, 1], I32)
        tok = sb("tok", [P, TC * E], I32)
        dst = sb("dst", [P, TC * E], I32)
        bank = [ctx.enter_context(nc.psum_tensor(f"bank{i}", [P, 512], F32)) for i in range(8)]

        ident, flip = C[:, C_ID:C_ID + P], V[:, 5376:5376 + P]
        tri, ones = C[:, C_TRI:C_TRI + P], C[:, C_ONE:C_ONE + P]
        x3 = X[:, :].rearrange("p (c n) -> p c n", c=TC)
        xn3 = XN[:, :].rearrange("p (c n) -> p c n", c=TC)
        ht3 = HT[:, :].rearrange("p (k s) -> p k s", k=KC)
        rw3 = rw[:, :].rearrange("p (k n) -> p k n", k=KC)
        vw = [D, GROUPS * HALF]
        val = [V[:, 0:TC * w].rearrange("p (c n) -> p c n", c=TC) for w in vw]

        qw = [D, GROUPS * HALF]
        q_d = [dram(f"q_scratch{l}", [S, qw[l]]) for l in range(LAYERS)]
        k_d = [dram(f"k_scratch{l}", [S, qw[l]]) for l in range(LAYERS)]
        fb_d = dram("bias_scratch", [H, FDIST])
        mod_d = dram("mod_scratch", [N_MOD * 4, P])
        xn_d = [dram(f"xn_scratch{l}", [S, D]) for l in range(LAYERS)]
        x1_d = dram("x1_scratch", [S, D])
        tab_d = [dram(f"slot_table{l}", [E * S, 1], I32) for l in range(LAYERS)]
        ys_d = [dram(f"expert_rows{l}", [2 * S, D]) for l in range(LAYERS)]

        w_in = [sem(f"w_in{i}") for i in range(RING)]
        mod_sum, mod_pe, mod_row = sem("mod_sum"), sem("mod_pe"), sem("mod_row")
        mod_out = [sem(f"mod_out{i}") for i in range(2)]
        const_in, x_in, vec_in, bias_in = sem("const_in"), sem("x_in"), sem("vec_in"), sem("bias_in")
        tab_in = sem("tab_in")
        setup_pe, setup_dve, setup_act = sem("setup_pe"), sem("setup_dve"), sem("setup_act")
        fb_out, hank_in = sem("fb_out"), sem("hank_in")
        dve_s, act_s, pool_s = sem("dve_step"), sem("act_step"), sem("pool_step")
        out_done = sem("out_done")
        PROJ = {0: [("q", 0), ("q", 1), ("k", 0), ("k", 1), ("v", 0), ("v", 1)],
                1: [("k", 0), ("k", 1), ("k", 2), ("v", 0), ("v", 1), ("v", 2), ("q", 0), ("q", 1), ("q", 2)]}
        PHASES = {0: [("qkv", 0, 6)], 1: [("kv", 0, 6), ("q", 6, 9)]}

        def staged_before(l, j):
            return TC * sum(kind != "v" for kind, _ in PROJ[l][:j])

        N_STAGED = [staged_before(l, len(PROJ[l])) for l in range(LAYERS)]
        counts = dict(
            mod_t_pe=2, mod_ready=2, mod_rows_in=32, bias_rows=2,
            ss_ready=TC, rms_arg=1, rms_root=1, xn_ready=TC, xt_pe=KC, ht_ready=KC,
            proj_pe=6 * TC, proj_free=6 * TC, sq_ready=4 * TC, q_arg=4 * TC, q_root=4 * TC, stage_ready=4 * TC,
            qk_pe=QK_CREDIT[0] + H * QK_STEPS[0], qk_t=H * QK_STEPS[0],
            s_pe=CREDIT + H * TC, logits=CREDIT + H * TC, exps=2 * H * TC, probs=H * TC,
            pt_pe=H * TC, pt=H * TC, o_pe=CREDIT + H * TC, o_out=CREDIT + H * TC,
            sub_sq=TC, sub_arg=TC + 1, sub_root=1, sub_ready=TC, ot_pe=KC, ot_ready=KC,
            wo_pe=2 * TC, y_added=2 * TC, ga_in=32, x_re_in=16, gf_in=32, gate_row=2,
            ss2=TC, arg2=1, root2=1, xn2=TC, xt2_pe=KC, ht2=KC, xn_out=16,
            rw_in=64, route_pe=1, route_e=2, route_e_done=2, picked=1, rank_pe=1, dest_ready=1,
            tab_scat=16 * 2 * TC, tab_back=16, tab_f=1, tab_pe=1, tok_ready=1, flag_ready=1, g_zero=1,
            xr_pe=2 * E, xr_t=2 * E, gu_pe=2 * E, silu=E, hid=E, hid_pe=CREDIT + E, hid_t=E, dn_pe=2 * E,
            y_evac=2 * E, scat_all=1, comb_free=TC, x_new=TC, x_out=16 * TC)
        pairs = dict(stage_out=16 * N_STAGED[0] // 2, stage_in=H // 2 * STAGE_DMAS[0],
                     gath=16 * E // 2, scat=16 * E // 2, rows_in=16 * TC // 2)
        sems = {n: sem(n) for n in counts}
        sems2 = {n: [sem(f"{n}{i}") for i in range(2)] for n in pairs}
        from_one = ["qk_t", "pt", "hid", "hid_t", "y_evac", "s_pe"]
        sm = [dict(**{n: Signal(sems[n], l * k + (n in from_one)) for n, k in counts.items()},
                              **{n: [Signal(x, l * k) for x in sems2[n]] for n, k in pairs.items()})
              for l in range(LAYERS)]
        ov_from_one = ["dn_pe", "xr_pe", "xr_t"]
        ov_names = ["w", "g", "xr_pe", "xr_t", "gu_pe", "silu", "hid", "hid_pe", "hid_t", "dn_pe", "y", "scat", "step"]
        ov = [dict(**{n: Signal(sem(f"ov_{n}_{l}"), int(n in ov_from_one)) for n in ov_names})
              for l in range(LAYERS)]

        def slot(n):
            return ring[:, n % RING, :]

        def slot3(n, k=KC):
            return slot(n).rearrange("p (k m) -> p k m", k=k)

        def arrived(eng, n, turn=0):
            eng.wait_ge(w_in[n % RING], turn * 16 + 16 * (n // RING + 1))

        def widths(l, c):
            return [(c + 1) * P] if l == 0 else [P * min(c + 1, 2), (c + 1) * P, (c + 1) * P]

        def expert_weights(l, e):
            g = t["moe_w_gate"][l, ds(e, 1)].rearrange("o (k p) n -> p (o k) n", p=P)
            u = t["moe_w_up"][l, ds(e, 1)].rearrange("o (k p) n -> p (o k) n", p=P)
            d = t["moe_w_down"][l, ds(e, 1)].rearrange("o (k p) n -> p (o k) n", p=P)
            return g, u, d

        n_norm = [1, 2]

        block = ctx.enter_context(nc.Block())

        @block.sync
        def _(sp):
            def used(n):
                kind, l, i = ORDER[n]
                s = sm[l]
                if kind == "mod":
                    sp.wait_ge(mod_sum, i + 1)
                elif kind == "proj":
                    sp.wait_ge(*s["proj_pe"](TC * (i + 1)))
                elif kind == "wo":
                    sp.wait_ge(*s["wo_pe"](TC * (i + 1) if l == 0 else 2 * TC))
                elif i in (0, 1):
                    sp.wait_ge(*s["gu_pe"](i + 1))
                elif i == MOE_BLOCKS - 1:
                    sp.wait_ge(*s["dn_pe"](2 * E))
                elif (i - 2) % 3 == 2:
                    sp.wait_ge(*s["dn_pe"](2 * ((i - 4) // 3) + 2))
                else:
                    sp.wait_ge(*s["gu_pe"](2 * ((i + 1) // 3) + 1 + (i + 1) % 3))

            def load(n, src, k=KC):
                if n >= RING:
                    used(n - RING)
                sp.dma_start(slot3(n, k), src).then_inc(w_in[n % RING], 16)

            def columns(w, b):
                return w[:, b * HALF:(b + 1) * HALF].rearrange("(k p) n -> p k n", p=P)

            sp.wait_ge(vec_in, 16 * N_VEC)
            for l in range(LAYERS):
                for n, (kind, layer, i) in enumerate(ORDER):
                    if layer != l or kind == "moe":
                        continue
                    if kind == "mod":
                        load(n, columns(t["kv_ada_w"], i - 12) if 12 <= i < 16 else
                             columns(t["ada_w"][i // 16], i % 16))
                    elif kind == "proj" and l == 0:
                        load(n, columns(t["a_w_qkv"][0], i))
                    elif kind == "proj":
                        load(n, columns(t["kv_w"], i) if i < 6 else columns(t["b_w_q"][0], i - 6))
                    elif l == 0:
                        load(n, columns(t["a_w_o"][0], i))
                    else:
                        load(n, t["b_w_o"][0].rearrange("(k p) n -> p k n", p=P), k=4)
                m = AT["moe", l, 0]
                g, u, _ = expert_weights(l, 0)
                load(m, g)
                load(m + 1, u)
                for e in range(2):
                    g, u, _ = expert_weights(l, e + 1)
                    load(m + 2 + 3 * e, g)
                    load(m + 3 + 3 * e, u)
                    load(m + 4 + 3 * e, expert_weights(l, e)[2], k=4)
                with sp.Fori(1, 15) as it:
                    for j in range(2):
                        e = it * 2 + j
                        g, u, _ = expert_weights(l, it * 2 + (j + 1))
                        _, _, d = expert_weights(l, e)
                        at = m + 2 + 3 * j
                        sp.wait_ge(*sm[l]["gu_pe"](e * 2 - 1))
                        sp.dma_start(slot3(at), g).then_inc(w_in[at % RING], 16)
                        sp.wait_ge(*sm[l]["gu_pe"](e * 2))
                        sp.dma_start(slot3(at + 1), u).then_inc(w_in[(at + 1) % RING], 16)
                        sp.wait_ge(*sm[l]["dn_pe"](e * 2 - 2))
                        sp.dma_start(slot3(at + 2, 4), d).then_inc(w_in[(at + 2) % RING], 16)
                g, u, _ = expert_weights(l, E - 1)
                load(m + 92, g)
                load(m + 93, u)
                load(m + 94, expert_weights(l, E - 2)[2], k=4)
                load(m + 95, expert_weights(l, E - 1)[2], k=4)
                sp.wait_ge(*sm[l]["flag_ready"](1))
                most = sp.value_load(flag[0:1, 0:1], min_val=0, max_val=S)
                with sp.If(most > P):
                    sp.wait_ge(*sm[l]["dn_pe"](2 * E))
                    for b in range(1, TC):
                        with sp.Fori(0, E) as e:
                            u0 = (b - 1) * E
                            g, u, d = expert_weights(l, e)
                            sp.wait_ge(*ov[l]["dn_pe"](e + u0))
                            sp.dma_start(slot3(0), g).then_inc(ov[l]["w"].sem, 16)
                            sp.dma_start(slot3(1), u).then_inc(ov[l]["w"].sem, 16)
                            sp.dma_start(slot3(2, 4), d).then_inc(ov[l]["w"].sem, 16)
                    sp.wait_ge(*ov[l]["dn_pe"]((TC - 1) * E))
            for c in range(TC):
                sp.wait_ge(*sm[1]["x_new"](c + 1))
                sp.dma_start(out[0, c * P:(c + 1) * P, :], x3[:, c, :]).then_inc(out_done, 16)
            sp.wait_ge(out_done, 16 * TC)

        @block.gpsimd
        def _(pool):
            step = Steps(pool, pool_s)
            for n in from_one:
                pool.sem_inc(sems[n], 1)
            for o in ov:
                for sig in (o["dn_pe"], o["xr_pe"], o["xr_t"]):
                    pool.sem_inc(sig.sem, 1)
            empty = V[:, 5120:5120 + P].bitcast(I32)
            step(pool.memset(empty, UNUSED))
            for l in range(LAYERS):
                pool.dma_start(tab_d[l].rearrange("(p n) o -> p (n o)", p=P), empty).then_inc(tab_in, 16)
            pool.wait_ge(setup_dve, 5)
            pool.dma_start(fb_d, W[0:H, 1024:1024 + FDIST]).then_inc(fb_out, 16)
            pool.wait_ge(fb_out, 16)
            hankel = bass.AP(fb_d.tensor, 0, [[1, P], [FDIST, H], [1, S]])
            pool.dma_start(V[:, 0:H * S].rearrange("p (h s) -> p h s", h=H), hankel).then_inc(hank_in, 16)

            for l in range(LAYERS):
                s, o = sm[l], ov[l]
                j = 0
                for kind, b in PROJ[l]:
                    if kind == "v":
                        continue
                    for c in range(TC):
                        pool.wait_ge(*s["stage_ready"](j + 1))
                        to = (q_d if kind == "q" else k_d)[l][c * P:(c + 1) * P, b * HALF:(b + 1) * HALF]
                        pool.dma_start(to, W[:, 1024 + HALF * (j % 2):1024 + HALF * (j % 2 + 1)]).then_inc(s["stage_out"][j % 2].sem, 16)
                        j += 1
                for i in range(2):
                    pool.wait_ge(*s["stage_out"][i](16 * (N_STAGED[l] // 2)))
                hw = P if l == 0 else GROUPS * DH
                with pool.Fori(0, H // 2) as it:
                    for b in range(2):
                        h = it * 2 + b
                        pool.wait_ge(*s["qk_pe"](it * 2 * QK_STEPS[l] + ((b - 1) * QK_STEPS[l] + QK_CREDIT[l])))
                        for i, d in enumerate((q_d[l], k_d[l])):
                            to = HT[:, (2 * b + i) * 768:(2 * b + i) * 768 + TC * hw]
                            if l == 0:
                                pool.dma_start(to.rearrange("p (c n) -> p c n", c=TC),
                                               d[:, ds(h * P, P)].rearrange("(c p) n -> p c n", p=P)).then_inc(s["stage_in"][b].sem, 16)
                            else:
                                for c in range(TC):
                                    pool.dma_start(
                                        to.rearrange("p (c g n) -> p c g n", c=TC, g=GROUPS)[:, c],
                                        d.rearrange("(c p) (g n) -> c p g n", p=P, g=GROUPS)[
                                            c, :, :, ds(h * DH, DH)]).then_inc(s["stage_in"][b].sem, 16)
                pool.wait_ge(*s["s_pe"](CREDIT + TC * H))
                xin = t["x"][0] if l == 0 else x1_d
                pool.dma_start(x3, xin.rearrange("(c p) n -> p c n", p=P)).then_inc(s["x_re_in"].sem, 16)
                pool.wait_ge(*s["o_pe"](CREDIT + TC * H))
                def gate_rows(to, col):
                    row = 64 * l + col // P
                    pool.dma_start(to[:, 0:D], mod_d[row:row + KC, :].rearrange("(o k) n -> o (k n)", o=1)
                                   .broadcast_to([P, D])).then_inc(s["ga_in" if col == 2 * D else "gf_in"].sem, 16)
                    pool.dma_start(to[:, D:2 * D], t["ada_b"][l:l + 1, col:col + D].broadcast_to([P, D])).then_inc(
                        s["ga_in" if col == 2 * D else "gf_in"].sem, 16)

                gate_rows(V, 2 * D)
                pool.dma_start(rw3[:, :, 0:NG], t["moe_w_group"][l].rearrange("(k p) n -> p k n", p=P)).then_inc(s["rw_in"].sem, 16)
                pool.dma_start(rw3[:, :, NG:NR], t["moe_w_expert"][l].rearrange("(k p) n -> p k n", p=P)).then_inc(s["rw_in"].sem, 16)
                pool.dma_start(rbias[:, 0:NG], t["moe_b_group"][l:l + 1, :].broadcast_to([P, NG])).then_inc(s["rw_in"].sem, 16)
                pool.dma_start(rbias[:, NG:NR], t["moe_b_expert"][l:l + 1, :].broadcast_to([P, E])).then_inc(s["rw_in"].sem, 16)
                pool.wait_ge(*s["xn2"](TC))
                pool.dma_start(xn_d[l].rearrange("(c p) n -> p c n", p=P), xn3).then_inc(s["xn_out"].sem, 16)
                pool.wait_ge(*s["y_added"](2 * TC))
                pool.memset(V[:, 0:2 * D], 0.0).then_inc(s["g_zero"].sem, 1)
                pool.wait_ge(tab_in, 32)
                pool.wait_ge(*s["dest_ready"](1))
                for j in range(2 * TC):
                    pool.indirect_dma_start(tab_d[l], bass.IndirectOffsetOnAxis(ap=dest[:, j:j + 1], axis=0),
                                            aid[:, j:j + 1], None, bounds_check=E * S - 1,
                                            oob_is_err=False).then_inc(s["tab_scat"].sem, 16)
                pool.wait_ge(*s["tab_scat"](16 * 2 * TC))
                for b in range(2):
                    pool.wait_ge(mod_out[b], 16 * (N_MOD // 2))
                pool.dma_start(W[0:E, 3072:3072 + S].bitcast(I32),
                               tab_d[l].rearrange("(e n) o -> e (n o)", e=E)).then_inc(s["tab_back"].sem, 16)
                pool.wait_ge(*s["tok_ready"](1))
                gate_rows(W, 5 * D)
                pool.wait_ge(*s["xn_out"](16))
                pool.wait_ge(*s["g_zero"](1))

                last_token, last_row = pool.to_reg(S - 1), pool.to_reg(2 * S - 1)

                def gather(col, b, signal):
                    step(pool.tensor_copy(tokc[:, b:b + 1], tok[:, ds(col, 1)]))
                    pool.tensor_tensor(pause[:, :], C[:, 0:1], C[:, 1:2], ALU.add)
                    pool.indirect_dma_start(V[:, b * D:(b + 1) * D], None, xn_d[l],
                                            bass.IndirectOffsetOnAxis(ap=tokc[:, b:b + 1], axis=0),
                                            bounds_check=last_token, oob_is_err=False).then_inc(signal, 16)

                def scatter(col, b, signal):
                    step(pool.tensor_copy(dstc[:, b:b + 1], dst[:, ds(col, 1)]))
                    pool.tensor_tensor(pause[:, :], C[:, 0:1], C[:, 1:2], ALU.add)
                    pool.indirect_dma_start(ys_d[l], bass.IndirectOffsetOnAxis(ap=dstc[:, b:b + 1], axis=0),
                                            HT[:, b * D:(b + 1) * D], None,
                                            bounds_check=last_row, oob_is_err=False).then_inc(signal, 16)

                gather(0, 0, s["gath"][0].sem)
                gather(1, 1, s["gath"][1].sem)

                def expert(e, b, more):
                    if more:
                        pool.wait_ge(*s["xr_pe"](e * 2 + 2))
                        gather(e + 2, b, s["gath"][b].sem)
                    pool.wait_ge(*s["y_evac"](e * 2 + 2))
                    scatter(e, b, s["scat"][b].sem)

                with pool.Fori(0, 15) as it:
                    step.enter(it, 4)
                    for b in range(2):
                        expert(it * 2 + b, b, True)
                    step.leave(15)
                for b in range(2):
                    expert(E - 2 + b, b, False)
                for b in range(2):
                    pool.wait_ge(*s["scat"][b](16 * (E // 2)))
                most = pool.value_load(flag[0:1, 0:1], min_val=0, max_val=S)
                with pool.If(most > P):
                    main_step, step = step, Steps(pool, o["step"].sem)
                    for b in range(1, TC):
                        with pool.Fori(0, E) as e:
                            step.enter(e, 2)
                            u0 = (b - 1) * E
                            pool.wait_ge(*o["xr_pe"](e * 2 + 2 * u0))
                            gather(e + b * E, 0, o["g"].sem)
                            pool.wait_ge(*o["y"](e * 2 + (2 * u0 + 2)))
                            scatter(e + b * E, 0, o["scat"].sem)
                            pool.wait_ge(*o["scat"](e * 16 + (16 * u0 + 16)))
                            step.leave(E)
                    step = main_step
                pool.sem_inc(s["scat_all"].sem, 1)
                for c in range(TC):
                    if c >= 2:
                        pool.wait_ge(*s["comb_free"](c - 1))
                    at = XN[:, (c % 2) * 2 * D:(c % 2 + 1) * 2 * D].rearrange("p (k n) -> p k n", k=2)
                    pool.dma_start(at, ys_d[l].rearrange("(k c p) n -> c p k n", k=2, p=P)[c]).then_inc(s["rows_in"][c % 2].sem, 16)
                if l == 0:
                    for c in range(TC):
                        pool.wait_ge(*s["x_new"](c + 1))
                        pool.dma_start(x1_d[c * P:(c + 1) * P, :], x3[:, c, :]).then_inc(s["x_out"].sem, 16)
                    pool.wait_ge(*s["x_out"](16 * TC))

        @block.scalar
        def _(act):
            act.dma_start(C[:, :], const).then_inc(const_in, 16)
            vecs = [(V_C, t["c"].rearrange("b (k p) -> (b k) p", p=P)),
                    (V_NA, t["norm_attn"].rearrange("l (k p) -> (l k) p", p=P)),
                    (V_NF, t["norm_ffn"].rearrange("l (k p) -> (l k) p", p=P)),
                    (V_KN, t["kv_norm"].rearrange("(k p) -> k p", p=P)),
                    (V_KAB, t["kv_ada_b"].rearrange("(k p) -> k p", p=P)),
                    (V_SUB, t["a_subln"])]
            for at, src in vecs:
                act.dma_start(W[at:at + src.shape[0], 0:P], src).then_inc(vec_in, 16)
            for at, src in ((V_QG, t["a_q_norm"]), (V_KG, t["a_k_norm"])):
                for i in range(2):
                    act.dma_start(W[at:at + 1, i * DH:(i + 1) * DH], src).then_inc(vec_in, 16)
            for at, src in ((V_BQ, t["b_q_norm"][0]), (V_BK, t["kv_k_norm"])):
                act.dma_start(W[at:at + 1, 0:P], src[0:2, :].rearrange("(o g) n -> o (g n)", o=1)).then_inc(vec_in, 16)
                for i in range(2):
                    act.dma_start(W[at + 1:at + 2, i * DH:(i + 1) * DH], src[2:3, :]).then_inc(vec_in, 16)
            act.dma_start(W[0:96, P:2 * P], t["ada_b"].rearrange("l (j p) -> (l j) p", p=P)).then_inc(vec_in, 16)
            act.dma_start(W[:, 256:512], t["a_lambda"].rearrange("o i n -> o (i n)").broadcast_to([P, 256])).then_inc(vec_in, 16)
            act.dma_start(W[:, 1792:1792 + M_END], masks[:, 0:M_END]).then_inc(vec_in, 16)
            act.dma_start(flip, masks[:, M_FLIP:M_FLIP + P]).then_inc(vec_in, 16)
            act.dma_start(V[0:BUCKETS + 1, 4096:4096 + FDIST], buckets).then_inc(bias_in, 16)
            act.dma_start(V[0:BUCKETS, 4096 + FDIST:4096 + FDIST + H], t["rel_bias"]).then_inc(bias_in, 16)
            act.dma_start(x3, t["x"][0].rearrange("(c p) n -> p c n", p=P)).then_inc(x_in, 16)
            act.wait_ge(setup_dve, 1)
            act.activation(cact[:, :], colV[:, V_C:V_C + KC], ACT.Silu).then_inc(setup_act, 1)
            act.wait_ge(setup_dve, 3)
            act.activation(lamw[:, 2:4], lamw[:, 0:2], ACT.Exp).then_inc(setup_act, 1)

            for l in range(LAYERS):
                s, o = sm[l], ov[l]

                def mod_row_out(i):
                    row = W[0:1, 3072:3072 + HALF] if i % 2 == 0 else V[0:1, 5504:5504 + HALF]
                    act.wait_ge(mod_pe, i + 1)
                    if i >= 2:
                        act.wait_ge(mod_out[i % 2], 16 * (i // 2))
                    act.activation(row, bank[4 + i % 2][0:1, :], ACT.Identity).then_inc(mod_row, 1)
                    act.wait_ge(mod_row, i + 1)
                    act.dma_start(mod_d[4 * i:4 * i + 4, :].rearrange("(o k) n -> o (k n)", o=1), row).then_inc(
                        mod_out[i % 2], 16)

                def mod_rows_in(i0, i1, n):
                    for b in range(2):
                        act.wait_ge(mod_out[b], 16 * (i1 // 2))
                    act.dma_start(W[0:4 * (i1 - i0), 3584:3584 + P], mod_d[4 * i0:4 * i1, :]).then_inc(
                        s["mod_rows_in"].sem, 16)

                if l == 0:
                    act.wait_ge(x_in, 16)
                else:
                    act.wait_ge(*sm[0]["x_new"](TC))
                for c in range(TC):
                    if c:
                        act.wait_ge(*s["ss_ready"](c))
                    act.activation(XN[:, 0:D], x3[:, c, :], ACT.Square,
                                   accum_out=small[:, c:c + 1]).then_inc(s["ss_ready"].sem, 1)
                act.wait_ge(*s["rms_arg"](1))
                act.activation(small[:, 8:12], small[:, 4:8], ACT.Sqrt).then_inc(s["rms_root"].sem, 1)
                if l == 0:
                    for i in range(4):
                        mod_row_out(i)
                    mod_rows_in(0, 4, 1)
                else:
                    mod_rows_in(12, N_MOD, 1)

                u = 0
                for phase, (kind, j0, j1) in enumerate(PHASES[l]):
                    a, sh = (2, kvm[:, 0:8]) if kind == "kv" else (0, mod[:, 0:8])
                    act.wait_ge(*s["mod_ready"](1))
                    for k in range(KC):
                        act.wait_ge(*s["xt_pe"](phase * KC + k + 1))
                        if phase and k == 0:
                            act.wait_ge(*s["proj_pe"](TC * j0))
                        act.activation(ht3[:, k, :], bank[4 + k % 4][:, :], ACT.Identity,
                                       bias=sh[:, k:k + 1], scale=scl[:, a, k:k + 1]).then_inc(s["ht_ready"].sem, 1)
                    for j in range(j0, j1):
                        for c in range(TC):
                            if PROJ[l][j][0] != "v":
                                n = staged_before(l, j) + c
                                act.wait_ge(*s["proj_pe"](u + 1))
                                if n >= 2:
                                    act.wait_ge(*s["q_arg"](n - 1))
                                act.activation(W[:, HALF * (n % 2):HALF * (n % 2 + 1)], bank[u % 4][:, :],
                                               ACT.Square).then_inc(s["sq_ready"].sem, 1)
                                act.wait_ge(*s["q_arg"](n + 1))
                                act.activation(small[:, 24:32], small[:, 16:24], ACT.Sqrt).then_inc(s["q_root"].sem, 1)
                            if l == 0 and u in mods_after("proj", 2):
                                mod_row_out(mods_after("proj", 2)[u])
                            u += 1
                if l == 0:
                    mod_row_out(21)
                    mod_rows_in(4, 12, 2)

                if l == 0:
                    kinds = [(V_QG, 0), (V_KG, 1)]
                else:
                    kinds = [(V_BQ, 0), (V_BK, 1), (V_BQ2, 2), (V_BK2, 3)]
                act.wait_ge(*s["proj_free"](TC * len(PROJ[l])))
                per = 2 * len(kinds)

                def part(it, n, i):
                    gain, at = kinds[i]
                    act.wait_ge(*s["qk_pe"](it * per + (n * len(kinds) + i + 1 + QK_CREDIT[l])))
                    if i == 0:
                        act.wait_ge(*s["s_pe"](it * 2 * TC + (CREDIT + TC * (n - 1))))
                    x0 = (4 * (n % 2) + at) * S
                    act.activation(X[:, x0:x0 + S], bank[0][:, :], ACT.Identity,
                                   scale=colV[:, gain:gain + 1]).then_inc(s["qk_t"].sem, 1)

                def exps(it, v):
                    c = v % TC
                    act.wait_ge(*s["logits"](it * 2 * TC + (v + 1 + CREDIT)))
                    if l == 0:
                        n = (c + 1) * P
                        for i in range(2):
                            at = (2 * (v % 2) + i) * S
                            act.activation(W[:, at:at + n], W[:, at:at + n], ACT.Exp,
                                           bias=small[:, 2 * (v % 2) + i:2 * (v % 2) + i + 1],
                                           accum_out=small2[:, 2 * (v % 2) + i:2 * (v % 2) + i + 1]).then_inc(s["exps"].sem, 1)
                    else:
                        n = sum(widths(l, c))
                        at = 1280 * (v % 2)
                        act.activation(W[:, at:at + n], W[:, at:at + n], ACT.Exp,
                                       bias=small[:, v % 2:v % 2 + 1],
                                       accum_out=small2[:, v % 2:v % 2 + 1]).then_inc(s["exps"].sem, 1)

                def probs_t(it, v):
                    c = v % TC
                    if l == 0:
                        n = (c + 1) * P
                        act.wait_ge(*s["pt_pe"](it * 2 * TC + (v + 1)))
                        act.wait_ge(*s["o_pe"](it * 2 * TC + (v - 1 + CREDIT)))
                        act.activation(W[:, 2048 + S * (v % 2):2048 + S * (v % 2) + n], bank[6][:, 0:n],
                                       ACT.Identity).then_inc(s["pt"].sem, 1)
                    else:
                        n = sum(widths(l, c))
                        act.wait_ge(*s["o_pe"](it * 2 * TC + (v + CREDIT)))
                        for r in range(ROUNDS[c]):
                            m = min(4 * P, n - r * 4 * P)
                            act.wait_ge(*s["pt_pe"](it * 2 * HEAD_ROUNDS + ((v // TC) * HEAD_ROUNDS + ROUND0[c] + r + 1)))
                            rr = (ROUND0[c] + r) % 2
                            act.activation(W[:, 2560 + r * 512:2560 + r * 512 + m], bank[5 + rr][:, 0:m],
                                           ACT.Identity).then_inc(s["pt"].sem, 1)

                def two_heads(it, last=False):
                    for v in range(2 * TC):
                        if v + 1 < 2 * TC or not last:
                            exps(it, v + 1)
                        probs_t(it, v)
                        if v // TC == 0 or not last:
                            for i in parts_after(l, v):
                                part(it, v // TC + 1, i)

                for i in range(len(kinds)):
                    part(0, 0, i)
                exps(0, 0)
                with act.Fori(0, H // 2 - 1) as it:
                    two_heads(it)
                two_heads(H // 2 - 1, last=True)

                if l == 0:
                    act.wait_ge(*s["o_out"](TC * H + CREDIT))
                    for c in range(TC):
                        if c >= 1:
                            act.wait_ge(*s["sub_arg"](c))
                        act.activation(W[:, 0:D], xn3[:, c, :], ACT.Square).then_inc(s["sub_sq"].sem, 1)
                    act.wait_ge(*s["sub_arg"](TC + 1))
                    act.activation(small2[:, 0:32], small[:, 0:32], ACT.Sqrt).then_inc(s["sub_root"].sem, 1)
                    for k in range(KC):
                        act.wait_ge(*s["ot_pe"](k + 1))
                        act.activation(ht3[:, k, :], bank[4 + k % 4][:, :], ACT.Identity,
                                       scale=colV[:, V_SUB:V_SUB + 1]).then_inc(s["ot_ready"].sem, 1)
                else:
                    for k in range(4):
                        act.wait_ge(*s["ot_pe"](k + 1))
                        act.activation(ht3[:, k, :], bank[4 + k % 4][:, :], ACT.Identity).then_inc(s["ot_ready"].sem, 1)

                if l == 0:
                    for u in range(2 * TC + 1):
                        if u in mods_after("wo", 2):
                            mod_row_out(mods_after("wo", 2)[u])
                for c in range(TC):
                    act.wait_ge(*s["y_added"](TC + c + 1))
                    if c:
                        act.wait_ge(*s["ss2"](c))
                    act.activation(W[:, 1024:1024 + D], x3[:, c, :], ACT.Square,
                                   accum_out=small[:, c:c + 1]).then_inc(s["ss2"].sem, 1)
                act.wait_ge(*s["arg2"](1))
                act.activation(small[:, 8:12], small[:, 4:8], ACT.Sqrt).then_inc(s["root2"].sem, 1)
                for k in range(KC):
                    act.wait_ge(*s["xt2_pe"](k + 1))
                    if k == 0:
                        act.wait_ge(*s["wo_pe"](2 * TC))
                    act.activation(ht3[:, k, :], bank[4 + k % 4][:, :], ACT.Identity,
                                   bias=mod[:, 24 + k:25 + k], scale=scl[:, 1, k:k + 1]).then_inc(s["ht2"].sem, 1)
                act.wait_ge(*s["route_e"](1))
                act.activation(small2[:, 20:36], small2[:, 20:36], ACT.Exp).then_inc(s["route_e_done"].sem, 1)
                act.wait_ge(*s["route_e"](2))
                act.activation(small2[:, 36:40], small2[:, 36:40], ACT.Exp).then_inc(s["route_e_done"].sem, 1)

                def rows_t(e, b):
                    for r in range(2):
                        act.wait_ge(*s["xr_pe"](e * 2 + (r + 1)))
                        if r == 0 and not (isinstance(e, int) and e < 2):
                            act.wait_ge(*s["gu_pe"](e * 2 - 2))
                        for q in range(4):
                            k = 4 * r + q
                            ins = act.activation(V[:, 2 * D + b * D + k * P:2 * D + b * D + (k + 1) * P],
                                                 bank[0][:, q * P:(q + 1) * P], ACT.Identity,
                                                 bias=mod[:, 24 + k:25 + k], scale=scl[:, 1, k:k + 1])
                        ins.then_inc(s["xr_t"].sem, 1)

                def silu(e, b):
                    act.wait_ge(*s["gu_pe"](e * 2 + 1))
                    act.wait_ge(*s["hid_pe"](e + (CREDIT - 1)))
                    act.activation(V[:, 4 * D + b * HALF:4 * D + (b + 1) * HALF], bank[2 + b][:, :],
                                   ACT.Silu).then_inc(s["silu"].sem, 1)

                def y_half(e, b):
                    act.wait_ge(*s["dn_pe"](e * 2 + 1))
                    act.wait_ge(*s["scat"][b]((e - b) * 8))
                    act.activation(HT[:, b * D:b * D + HALF], bank[6][:, :], ACT.Identity).then_inc(s["y_evac"].sem, 1)

                rows_t(0, 0)
                rows_t(1, 1)
                silu(0, 0)

                def expert(e, b):
                    silu(e + 1, 1 - b)
                    rows_t(e + 2, b)
                    y_half(e, b)

                for b in range(2):
                    expert(b, b)
                with act.Fori(1, 15) as it:
                    for b in range(2):
                        expert(it * 2 + b, b)
                silu(E - 1, 1)
                y_half(E - 2, 0)
                y_half(E - 1, 1)

                act.wait_ge(*s["flag_ready"](1))
                most = act.value_load(flag[0:1, 0:1], min_val=0, max_val=S)
                with act.If(most > P):
                    for bb in range(1, TC):
                        with act.Fori(0, E) as e:
                            u0 = (bb - 1) * E
                            for r in range(2):
                                act.wait_ge(*o["xr_pe"](e * 2 + (2 * u0 + r + 1)))
                                for q in range(4):
                                    k = 4 * r + q
                                    ins = act.activation(V[:, 2 * D + k * P:2 * D + (k + 1) * P],
                                                         bank[0][:, q * P:(q + 1) * P], ACT.Identity,
                                                         bias=mod[:, 24 + k:25 + k], scale=scl[:, 1, k:k + 1])
                                ins.then_inc(o["xr_t"].sem, 1)
                            act.wait_ge(*o["gu_pe"](e * 2 + (2 * u0 + 1)))
                            act.activation(V[:, 4 * D:4 * D + HALF], bank[2][:, :], ACT.Silu).then_inc(o["silu"].sem, 1)
                            act.wait_ge(*o["dn_pe"](e + (u0 + 1)))
                            act.activation(HT[:, 0:HALF], bank[6][:, :], ACT.Identity).then_inc(o["y"].sem, 1)

        @block.vector
        def _(dve):
            step = Steps(dve, dve_s)
            dve.wait_ge(setup_pe, 1)
            dve.tensor_copy(colV[:, :], bank[0][:, 0:V_END]).then_inc(setup_dve, 1)
            dve.wait_ge(setup_dve, 1)
            step(dve.tensor_scalar(colV[:, V_QG:V_QG + 1], colV[:, V_QG:V_QG + 1], DH ** -0.5, None, ALU.mult))
            step(dve.tensor_scalar(colV[:, V_BQ:V_BQ + 2], colV[:, V_BQ:V_BQ + 2], DH ** -0.5, None, ALU.mult))
            step(dve.tensor_scalar(colV[:, V_SUB:V_SUB + 1], colV[:, V_SUB:V_SUB + 1], 1 - LAM_INIT, None, ALU.mult))
            dve.wait_ge(setup_pe, 2)
            dve.tensor_copy(colA[:, :], bank[1][:, 0:96]).then_inc(setup_dve, 1)
            lp = W[:, 256:512].rearrange("p (a i n) -> p a i n", a=2, i=2)
            step(dve.tensor_tensor(W[:, 512:640].rearrange("p (a n) -> p a n", a=2),
                                   lp[:, :, 0, :], lp[:, :, 1, :], ALU.mult))
            dve.tensor_reduce(lamw[:, 0:2], W[:, 512:640].rearrange("p (a n) -> p a n", a=2), AX.X,
                              ALU.add).then_inc(setup_dve, 1)
            step(dve.tensor_copy(maskb[:, :], W[:, 1792:1792 + M_END]))
            dve.wait_ge(const_in, 16)
            step(dve.tensor_copy(identb[:, :], ident))
            step(dve.tensor_copy(aid[:, :], C[:, C_AID:C_AID + 2 * TC]))
            dve.wait_ge(setup_act, 2)
            step(dve.tensor_tensor(lamw[:, 4:5], lamw[:, 3:4], lamw[:, 2:3], ALU.subtract))
            step(dve.tensor_scalar(nlam[:, :], lamw[:, 4:5], LAM_INIT, None, ALU.subtract))
            dve.wait_ge(bias_in, 32)
            dve.memset(V[BUCKETS:BUCKETS + 1, 4096 + FDIST:4096 + FDIST + H], NEG).then_inc(setup_dve, 1)
            dve.wait_ge(setup_pe, 3)
            step(dve.tensor_copy(W[0:H, 1024:1024 + 512], bank[2][0:H, :]))
            dve.tensor_copy(W[0:H, 1536:1536 + P], bank[3][0:H, 0:P]).then_inc(setup_dve, 1)

            for l in range(LAYERS):
                s, o = sm[l], ov[l]

                def norm(sq, arg, root, ready):
                    dve.wait_ge(*sq(TC))
                    dve.tensor_scalar(small[:, 4:8], small[:, 0:4], 1.0 / D, EPS, ALU.mult, ALU.add).then_inc(arg.sem, 1)
                    dve.wait_ge(*root(1))
                    step(dve.reciprocal(small[:, 12:16], small[:, 8:12]))
                    for c in range(TC):
                        dve.tensor_scalar(xn3[:, c, :], x3[:, c, :], small[:, 12 + c:13 + c], None,
                                          ALU.mult).then_inc(ready.sem, 1)

                def mod_sums(i):
                    acc = W[:, 2048 + HALF * (i % 2):2048 + HALF * (i % 2 + 1)]
                    n = AT["mod", 0, i]
                    arrived(dve, n)
                    if i >= 2:
                        dve.wait_ge(mod_pe, i - 1)
                    step(dve.tensor_scalar(acc, slot3(n)[:, 0, :], cact[:, 0:1], None, ALU.mult))
                    for k in range(1, KC):
                        ins = dve.scalar_tensor_tensor(acc, slot3(n)[:, k, :], cact[:, k:k + 1], acc,
                                                       ALU.mult, ALU.add)
                        if k < KC - 1:
                            step(ins)
                    ins.then_inc(mod_sum, 1)

                norm(s["ss_ready"], s["rms_arg"], s["rms_root"], s["xn_ready"])
                if l == 0:
                    dve.wait_ge(fb_out, 16)
                    dve.wait_ge(setup_act, 1)
                    for i in range(4):
                        mod_sums(i)

                def modulation(cols, bias_col):
                    ins = dve.tensor_tensor(mod[:, cols], bank[0][:, bias_col:bias_col + cols.stop - cols.start],
                                            colA[:, l * 48 + cols.start:l * 48 + cols.stop], ALU.add)
                    step(ins)

                def scales(which, at, gain):
                    return dve.scalar_tensor_tensor(scl[:, which, :], at, 1.0, colV[:, gain:gain + KC],
                                                    ALU.add, ALU.mult)

                u = 0
                for phase, (kind, j0, j1) in enumerate(PHASES[l]):
                    if phase == 0:
                        dve.wait_ge(*s["mod_t_pe"](1))
                        if l == 0:
                            modulation(slice(0, 16), 0)
                        else:
                            step(dve.tensor_tensor(kvm[:, :], bank[0][:, 0:16], colV[:, V_KAB:V_KAB + 16], ALU.add))
                            modulation(slice(0, 48), 16)
                            step(scales(2, kvm[:, 8:16], V_KN))
                            step(scales(1, mod[:, 32:40], V_NF + l * KC))
                        scales(0, mod[:, 8:16], V_NA + l * KC).then_inc(s["mod_ready"].sem, 1)
                    for j in range(j0, j1):
                        kd, b = PROJ[l][j]
                        for c in range(TC):
                            if kd == "v":
                                dve.wait_ge(*s["proj_pe"](u + 1))
                                dve.tensor_copy(val[l][:, c, b * HALF:(b + 1) * HALF],
                                                bank[u % 4][:, :]).then_inc(s["proj_free"].sem, 1)
                            else:
                                n = staged_before(l, j) + c
                                dve.wait_ge(*s["sq_ready"](n + 1))
                                step(dve.tensor_reduce(small2[:, 0:8],
                                                       W[:, HALF * (n % 2):HALF * (n % 2 + 1)].rearrange(
                                                           "p (a n) -> p a n", n=DH), AX.X, ALU.add))
                                dve.tensor_scalar(small[:, 16:24], small2[:, 0:8], 1.0 / DH, EPS,
                                                  ALU.mult, ALU.add).then_inc(s["q_arg"].sem, 1)
                                dve.wait_ge(*s["q_root"](n + 1))
                                step(dve.reciprocal(small2[:, 8:16], small[:, 24:32]))
                                if n >= 2:
                                    dve.wait_ge(*s["stage_out"][n % 2](16 * (n // 2)))
                                at = W[:, 1024 + HALF * (n % 2):1024 + HALF * (n % 2 + 1)]
                                ins = dve.tensor_tensor(at.rearrange("p (a n) -> p a n", n=DH),
                                                        bank[u % 4][:, :].rearrange("p (a n) -> p a n", n=DH),
                                                        small2[:, 8:16].unsqueeze(2).broadcast_to([P, 8, DH]),
                                                        ALU.mult)
                                ins.then_inc(s["stage_ready"].sem, 1)
                                dve.wait_ge(*s["stage_ready"](n + 1))
                                dve.sem_inc(s["proj_free"].sem, 1)
                            if l == 0 and u in mods_after("proj"):
                                mod_sums(mods_after("proj")[u])
                            if l == 0 and u == 0:
                                for h in range(H):
                                    dve.wait_ge(setup_pe, 4 + h)
                                    dve.tensor_copy(T[:, h * S:(h + 1) * S], bank[6 + h % 2][:, :]).then_inc(
                                        setup_dve, 1)
                            u += 1
                if l == 0:
                    dve.wait_ge(*s["mod_t_pe"](2))
                    modulation(slice(16, 48), 0)
                    scales(1, mod[:, 32:40], V_NF).then_inc(s["mod_ready"].sem, 1)

                for i in range(2):
                    dve.wait_ge(*s["stage_out"][i](16 * (N_STAGED[l] // 2)))
                if l == 0:
                    dve.wait_ge(setup_dve, 13)
                dve.sem_inc(s["logits"].sem, CREDIT)
                dve.sem_inc(s["o_out"].sem, CREDIT)

                def logits(it, v):
                    c = v % TC
                    h = it * 2 + v // TC
                    n = (c + 1) * P
                    dve.wait_ge(*s["s_pe"](it * 2 * TC + (v + 1 + CREDIT)))
                    if l == 0:
                        if v >= 2:
                            dve.wait_ge(*s["pt_pe"](it * 2 * TC + (v - 1)))
                        for i in range(2):
                            at = (2 * (v % 2) + i) * S
                            ins = dve.tensor_tensor(W[:, at:at + n], bank[2 + 2 * (v % 2) + i][:, 0:n],
                                                    T[:, ds(h * S + (S - n), n)], ALU.add)
                        step(ins)
                        at = 2 * (v % 2) * S
                        dve.tensor_reduce(small[:, 2 * (v % 2):2 * (v % 2) + 2],
                                          W[:, at:at + 2 * S].rearrange("p (i n) -> p i n", i=2)[:, :, 0:n],
                                          AX.X, ALU.max, negate=True).then_inc(s["logits"].sem, 1)
                    else:
                        if v >= 2:
                            dve.wait_ge(*s["pt_pe"](it * 2 * HEAD_ROUNDS + (
                                ((v - 2) // TC) * HEAD_ROUNDS + ROUND0[(v - 2) % TC] + ROUNDS[(v - 2) % TC])))
                        at = 1280 * (v % 2)
                        for g, w in enumerate(widths(l, c)):
                            ins = dve.tensor_tensor(W[:, at:at + w], bank[2 + g][:, 0:w],
                                                    T[:, ds(h * S + (S - w), w)], ALU.add)
                            at += w
                        step(ins)
                        dve.tensor_reduce(small[:, v % 2:v % 2 + 1], W[:, 1280 * (v % 2):at], AX.X, ALU.max,
                                          negate=True).then_inc(s["logits"].sem, 1)

                def probs(it, v):
                    c, b = v % TC, v % 2
                    n = (c + 1) * P
                    dve.wait_ge(*s["o_out"](it * 2 * TC + (v - 1 + CREDIT)))
                    if l == 0:
                        dve.wait_ge(*s["exps"](it * 4 * TC + (2 * v + 2)))
                        step(dve.reciprocal(small2[:, 8 + 2 * b:10 + 2 * b], small2[:, 2 * b:2 * b + 2]))
                        step(dve.tensor_scalar(small2[:, 12:13], small2[:, 9 + 2 * b:10 + 2 * b],
                                               small2[:, 2 * b:2 * b + 1], nlam[:, 0:1], ALU.mult, ALU.mult))
                        at = 2 * b * S
                        dve.scalar_tensor_tensor(W[:, at:at + n], W[:, at + S:at + S + n], small2[:, 12:13],
                                                 W[:, at:at + n], ALU.mult, ALU.add).then_inc(s["probs"].sem, 1)
                    else:
                        dve.wait_ge(*s["exps"](it * 2 * TC + (v + 1)))
                        step(dve.reciprocal(small2[:, 8 + 2 * b:9 + 2 * b], small2[:, b:b + 1]))

                def output(it, v):
                    c, b = v % TC, v % 2
                    h = it * 2 + v // TC
                    w = P if l == 0 else DH
                    dve.wait_ge(*s["o_pe"](it * 2 * TC + (v + 1 + CREDIT)))
                    to = XN[:, 0:TC * H * w].rearrange("p (c n) -> p c n", c=TC)[:, c, ds(h * w, w)]
                    dve.tensor_scalar(to, bank[O_BANK[v % 2]][:, 0:w], small2[:, 8 + 2 * b:9 + 2 * b],
                                      None, ALU.mult).then_inc(s["o_out"].sem, 1)

                def two_heads(it, last=False):
                    for v in range(2 * TC):
                        if l == 1:
                            probs(it, v)
                        elif v + 1 < 2 * TC or not last:
                            probs(it, v + 1)
                        if v + 2 < 2 * TC or not last:
                            logits(it, v + 2)
                        output(it, v)

                logits(0, 0)
                if l == 0:
                    probs(0, 0)
                logits(0, 1)
                with dve.Fori(0, H // 2 - 1) as it:
                    step.enter(it, 2 * TC * (3 if l == 0 else 2))
                    two_heads(it)
                    step.leave(H // 2 - 1)
                two_heads(H // 2 - 1, last=True)

                if l == 0:
                    dve.wait_ge(*s["o_out"](CREDIT + TC * H))
                    for c in range(TC):
                        dve.wait_ge(*s["sub_sq"](c + 1))
                        dve.tensor_reduce(small2[:, c * H:(c + 1) * H],
                                          W[:, 0:D].rearrange("p (h n) -> p h n", h=H), AX.X, ALU.add).then_inc(s["sub_arg"].sem, 1)
                    dve.wait_ge(*s["sub_arg"](TC))
                    dve.tensor_scalar(small[:, 0:32], small2[:, 0:32], 1.0 / P, EPS, ALU.mult, ALU.add).then_inc(s["sub_arg"].sem, 1)
                    dve.wait_ge(*s["sub_root"](1))
                    step(dve.reciprocal(small[:, 0:32], small2[:, 0:32]))
                    for c in range(TC):
                        v3 = xn3[:, c, :].rearrange("p (h n) -> p h n", h=H)
                        dve.tensor_tensor(v3, v3, small[:, c * H:(c + 1) * H].unsqueeze(2).broadcast_to([P, H, P]),
                                          ALU.mult).then_inc(s["sub_ready"].sem, 1)

                dve.wait_ge(*s["x_re_in"](16))
                dve.wait_ge(*s["ga_in"](32))
                step(dve.tensor_tensor(V[:, 0:D], V[:, 0:D], V[:, D:2 * D], ALU.add))
                for u in range(2 * TC):
                    hf, c = divmod(u, TC)
                    cols = slice(hf * HALF, (hf + 1) * HALF)
                    dve.wait_ge(*s["wo_pe"](u + 1))
                    step(dve.tensor_tensor(W[:, 0:HALF], bank[u % 4][:, :], V[:, cols], ALU.mult))
                    dve.tensor_tensor(x3[:, c, cols], x3[:, c, cols], W[:, 0:HALF], ALU.add).then_inc(s["y_added"].sem, 1)
                    dve.wait_ge(*s["y_added"](u + 1))
                    if l == 0 and u in mods_after("wo"):
                        mod_sums(mods_after("wo")[u])
                norm(s["ss2"], s["arg2"], s["root2"], s["xn2"])

                dve.wait_ge(*s["route_pe"](1))
                dve.wait_ge(*s["rw_in"](64))
                LG = W[:, 0:TC * NR].rearrange("p (c n) -> p c n", c=TC)
                gl, el = LG[:, :, 0:NG], LG[:, :, NG:NR]
                EQ = W[:, 144:272].rearrange("p (c n) -> p c n", c=TC)
                EQG = W[:, 144:160].rearrange("p (c n) -> p c n", c=TC)
                OH = [W[:, 272 + 128 * i:400 + 128 * i].rearrange("p (c n) -> p c n", c=TC) for i in range(2)]
                EM = W[:, 528:656].rearrange("p (c n) -> p c n", c=TC)
                M3 = W[:, 656:784].rearrange("p (c n) -> p c n", c=TC)
                RK = W[:, 784:912].rearrange("p (c n) -> p c n", c=TC)
                DF = W[:, 912:920]
                gmax, gidx, m1, i1, m2, i2 = (small2[:, 0:4], small2[:, 4:8], small2[:, 8:12], small2[:, 12:16],
                                              small2[:, 16:20], small[:, 0:4])
                eg = small2[:, 20:36].rearrange("p (c n) -> p c n", c=TC)
                e21 = small2[:, 36:40]
                gsum, gw, den, p1 = small[:, 4:8], small[:, 8:12], small[:, 12:16], small[:, 16:20]
                pen = small[:, 20:36]
                pen3 = pen.rearrange("p (c n) -> p c n", c=TC)

                def over(a, n):
                    return a.unsqueeze(2).broadcast_to([P, TC, n])

                def per_chunk(a, n):
                    return a.unsqueeze(1).broadcast_to([P, TC, n])

                step(dve.tensor_tensor(LG, bank[0][:, 0:TC * NR].rearrange("p (c n) -> p c n", c=TC),
                                       per_chunk(rbias[:, :], NR), ALU.add))
                iog, ioe = per_chunk(C[:, C_IG:C_IG + NG], NG), per_chunk(C[:, C_IE:C_IE + E], E)
                step(dve.tensor_reduce(gmax, gl, AX.X, ALU.max))
                step(dve.tensor_tensor(EQG, gl, over(gmax, NG), ALU.is_equal))
                step(dve.tensor_tensor(EQG, EQG, iog, ALU.mult))
                step(dve.tensor_reduce(gidx, EQG, AX.X, ALU.min))
                step(dve.tensor_tensor(pen3, iog, over(gidx, NG), ALU.is_equal))
                dve.tensor_tensor(eg, gl, over(gmax, NG), ALU.subtract).then_inc(s["route_e"].sem, 1)
                step(dve.tensor_scalar(pen, pen, -NEG, NEG, ALU.mult, ALU.add))
                step(dve.tensor_tensor(EM.rearrange("p c (g n) -> p c g n", g=NG),
                                       el.rearrange("p c (g n) -> p c g n", g=NG),
                                       pen3.unsqueeze(3).broadcast_to([P, TC, NG, PER_G]), ALU.add))
                for i, (m, ix) in enumerate(((m1, i1), (m2, i2))):
                    step(dve.tensor_reduce(m, EM, AX.X, ALU.max))
                    step(dve.tensor_tensor(EQ, EM, over(m, E), ALU.is_equal))
                    step(dve.tensor_tensor(EQ, EQ, ioe, ALU.mult))
                    step(dve.tensor_reduce(ix, EQ, AX.X, ALU.min))
                    step(dve.tensor_tensor(OH[i], ioe, over(ix, E), ALU.is_equal))
                    if i == 0:
                        step(dve.scalar_tensor_tensor(EM, OH[0], 2 * NEG, EM, ALU.mult, ALU.add))
                dve.tensor_tensor(M3, OH[0], OH[1], ALU.add).then_inc(s["picked"].sem, 1)
                dve.tensor_tensor(e21, m2, m1, ALU.subtract).then_inc(s["route_e"].sem, 1)
                dve.wait_ge(*s["route_e_done"](1))
                step(dve.tensor_reduce(gsum, eg, AX.X, ALU.add))
                step(dve.reciprocal(gw, gsum))
                dve.wait_ge(*s["route_e_done"](2))
                step(dve.tensor_scalar(den, e21, 1.0, None, ALU.add))
                step(dve.reciprocal(p1, den))
                step(dve.tensor_tensor(gates[:, 0, :], p1, gw, ALU.mult))
                step(dve.tensor_tensor(gates[:, 1, :], gates[:, 0, :], e21, ALU.mult))
                dve.wait_ge(*s["rank_pe"](1))
                step(dve.tensor_tensor(RK, bank[1][:, 0:TC * E].rearrange("p (c n) -> p c n", c=TC),
                                       per_chunk(C[:, C_E512:C_E512 + E], E), ALU.add))
                step(dve.tensor_reduce(DF[:, 0:1], bank[1][:, TC * E:TC * E + E], AX.X, ALU.max))
                dve.tensor_copy(flag[:, :], DF[:, 0:1]).then_inc(s["flag_ready"].sem, 1)
                dve.wait_ge(*s["flag_ready"](1))
                for i in range(2):
                    step(dve.tensor_tensor(EQ, OH[i], RK, ALU.mult))
                    step(dve.tensor_reduce(DF[:, 4 * i:4 * i + 4], EQ, AX.X, ALU.add))
                dve.tensor_copy(dest[:, :], DF).then_inc(s["dest_ready"].sem, 1)
                dve.wait_ge(*s["tab_back"](16))
                dve.tensor_copy(W[0:E, 2560:2560 + S], W[0:E, 3072:3072 + S].bitcast(I32)).then_inc(s["tab_f"].sem, 1)
                dve.wait_ge(*s["tab_pe"](1))
                step(dve.tensor_copy(dst[:, :], bank[2][:, 0:P]))
                step(dve.tensor_scalar(W[:, 1024:1024 + P], bank[2][:, 0:P], float(S), float(-S), ALU.is_ge, ALU.mult))
                dve.tensor_tensor(tok[:, :], bank[2][:, 0:P], W[:, 1024:1024 + P], ALU.add).then_inc(s["tok_ready"].sem, 1)

                def hidden(e, b):
                    dve.wait_ge(*s["silu"](e + 1))
                    dve.wait_ge(*s["gu_pe"](e * 2 + 2))
                    at = V[:, 4 * D + b * HALF:4 * D + (b + 1) * HALF]
                    dve.tensor_tensor(at, at, bank[4 + b][:, :], ALU.mult).then_inc(s["hid"].sem, 1)

                def hidden_t(e, b):
                    dve.wait_ge(*s["hid_pe"](e + (1 + CREDIT)))
                    if not (isinstance(e, int) and e < 2):
                        dve.wait_ge(*s["dn_pe"](e * 2 - 2))
                    dve.tensor_copy(V[:, 5 * D + b * HALF:5 * D + (b + 1) * HALF], bank[1][:, :]).then_inc(s["hid_t"].sem, 1)

                def y_half(e, b):
                    dve.wait_ge(*s["dn_pe"](e * 2 + 2))
                    dve.wait_ge(*s["y_evac"](e * 2 + 1))
                    dve.wait_ge(*s["scat"][b]((e - b) * 8))
                    dve.tensor_copy(HT[:, b * D + HALF:(b + 1) * D], bank[7][:, :]).then_inc(s["y_evac"].sem, 1)

                hidden(0, 0)
                hidden_t(0, 0)
                hidden(1, 1)
                y_half(0, 0)
                hidden_t(1, 1)
                hidden(2, 0)
                y_half(1, 1)
                with dve.Fori(1, 15) as it:
                    for b in range(2):
                        e = it * 2 + b
                        hidden_t(e, b)
                        hidden(e + 1, 1 - b)
                        y_half(e, b)
                hidden_t(E - 2, 0)
                hidden(E - 1, 1)
                y_half(E - 2, 0)
                hidden_t(E - 1, 1)
                y_half(E - 1, 1)

                most = dve.value_load(flag[0:1, 0:1], min_val=0, max_val=S)
                with dve.If(most > P):
                    for bb in range(1, TC):
                        with dve.Fori(0, E) as e:
                            u0 = (bb - 1) * E
                            dve.wait_ge(*o["silu"](e + (u0 + 1)))
                            dve.wait_ge(*o["gu_pe"](e * 2 + (2 * u0 + 2)))
                            at = V[:, 4 * D:4 * D + HALF]
                            dve.tensor_tensor(at, at, bank[4][:, :], ALU.mult).then_inc(o["hid"].sem, 1)
                            dve.wait_ge(*o["hid_pe"](e + (u0 + 1)))
                            dve.tensor_copy(V[:, 5 * D:5 * D + HALF], bank[1][:, :]).then_inc(o["hid_t"].sem, 1)
                            dve.wait_ge(*o["y"](e * 2 + (2 * u0 + 1)))
                            dve.tensor_copy(HT[:, HALF:D], bank[7][:, :]).then_inc(o["y"].sem, 1)

                dve.wait_ge(*s["gf_in"](32))
                step(dve.tensor_tensor(W[:, 0:D], W[:, 0:D], W[:, D:2 * D], ALU.add))
                for c in range(TC):
                    dve.wait_ge(*s["rows_in"][c % 2](16 * (c // 2 + 1)))
                    r0 = XN[:, (c % 2) * 2 * D:(c % 2) * 2 * D + D]
                    r1 = XN[:, (c % 2) * 2 * D + D:(c % 2 + 1) * 2 * D]
                    step(dve.tensor_scalar(r0, r0, gates[:, 0, c:c + 1], None, ALU.mult))
                    step(dve.scalar_tensor_tensor(r0, r1, gates[:, 1, c:c + 1], r0, ALU.mult, ALU.add))
                    step(dve.tensor_tensor(r0, r0, W[:, 0:D], ALU.mult))
                    dve.tensor_tensor(x3[:, c, :], x3[:, c, :], r0, ALU.add).then_inc(s["x_new"].sem, 1)
                    dve.wait_ge(*s["x_new"](c + 1))
                    dve.sem_inc(s["comb_free"].sem, 1)

        @block.tensor
        def _(pe):
            pe.wait_ge(const_in, 16)
            pe.wait_ge(vec_in, 16 * N_VEC)
            pe.transpose(bank[0][:, 0:V_END], W[0:V_END, 0:P], ident[0:V_END, 0:V_END]).then_inc(setup_pe, 1)
            pe.transpose(bank[1][:, 0:96], W[0:96, P:2 * P], ident[0:96, 0:96]).then_inc(setup_pe, 1)
            pe.wait_ge(setup_dve, 4)
            rel = V[0:BUCKETS + 1, 4096 + FDIST:4096 + FDIST + H]
            pe.matmul(bank[2][0:H, :], rel, V[0:BUCKETS + 1, 4096:4096 + 512], start=True, stop=True)
            pe.matmul(bank[3][0:H, 0:P], rel, V[0:BUCKETS + 1, 4608:4608 + P], start=True, stop=True).then_inc(setup_pe, 1)

            def mod_reduce(i):
                pe.wait_ge(mod_sum, i + 1)
                if i >= 2:
                    pe.wait_ge(mod_row, i - 1)
                pe.matmul(bank[4 + i % 2][0:1, :], ones[:, 0:1], W[:, 2048 + HALF * (i % 2):2048 + HALF * (i % 2 + 1)],
                          start=True, stop=True).then_inc(mod_pe, 1)

            def mod_columns(n, turn):
                pe.wait_ge(*s["mod_rows_in"](16 * turn))
                pe.transpose(bank[0][:, 0:n], W[0:n, 3584:3584 + P], ident[0:n, 0:n]).then_inc(s["mod_t_pe"].sem, 1)

            for i in range(4):
                mod_reduce(i)

            for l in range(LAYERS):
                s, o = sm[l], ov[l]
                u = 0
                for phase, (kind, j0, j1) in enumerate(PHASES[l]):
                    if phase == 0:
                        mod_columns(16 if l == 0 else 64, 1)
                        pe.wait_ge(*s["xn_ready"](TC))
                        if l == 0:
                            pe.wait_ge(mod_row, 4)
                    for k in range(KC):
                        if phase * KC + k >= 4:
                            pe.wait_ge(*s["ht_ready"](phase * KC + k - 3))
                        for c in range(TC):
                            ins = pe.transpose(bank[4 + k % 4][:, c * P:(c + 1) * P], xn3[:, c, k * P:(k + 1) * P], ident)
                        ins.then_inc(s["xt_pe"].sem, 1)
                    if phase == 0:
                        pe.wait_ge(*s["mod_ready"](1))
                    for j in range(j0, j1):
                        n = AT["proj", l, j]
                        arrived(pe, n)
                        for c in range(TC):
                            if u >= 4:
                                pe.wait_ge(*s["proj_free"](u - 3))
                            for k in range(KC):
                                if j == j0 and c == 0:
                                    pe.wait_ge(*s["ht_ready"](phase * KC + k + 1))
                                ins = pe.matmul(bank[u % 4][:, :], ht3[:, k, c * P:(c + 1) * P], slot3(n)[:, k, :],
                                                start=(k == 0), stop=(k == KC - 1))
                            ins.then_inc(s["proj_pe"].sem, 1)
                            if l == 0 and u == 0:
                                pe.wait_ge(hank_in, 16)
                                pe.wait_ge(*s["ht_ready"](KC))
                                for h in range(H):
                                    if h >= 2:
                                        pe.wait_ge(setup_dve, 4 + h)
                                    pe.matmul(bank[6 + h % 2][:, :], flip, V[:, h * S:(h + 1) * S], start=True,
                                              stop=True).then_inc(setup_pe, 1)
                            if l == 0 and u in mods_after("proj", 2):
                                mod_reduce(mods_after("proj", 2)[u])
                            u += 1
                    pe.wait_ge(*s["proj_free"](u))
                if l == 0:
                    mod_reduce(21)
                    mod_columns(32, 2)
                    pe.wait_ge(*s["mod_ready"](2))
                    pe.wait_ge(mod_row, 22)

                pe.sem_inc(s["qk_pe"].sem, QK_CREDIT[l])
                pe.sem_inc(s["s_pe"].sem, CREDIT)
                pe.sem_inc(s["o_pe"].sem, CREDIT)
                hw = P if l == 0 else GROUPS * DH
                parts = [(0, 0), (1, 0)] if l == 0 else [(0, 0), (1, 0), (0, DH), (1, DH)]
                nparts = len(parts)

                def part(it, n, i):
                    if i == 0:
                        pe.wait_ge(*s["stage_in"][n % 2](it * STAGE_DMAS[l] + (n // 2 + 1) * STAGE_DMAS[l]))
                    pe.wait_ge(*s["qk_t"](it * 2 * nparts + (n * nparts + i)))
                    qk, c0 = parts[i]
                    h0 = (2 * (n % 2) + qk) * 768
                    src = HT[:, h0:h0 + TC * hw].rearrange("p (c n) -> p c n", c=TC)
                    for c in range(TC):
                        ins = pe.transpose(bank[0][:, c * P:(c + 1) * P], src[:, c, c0:c0 + P], ident)
                    ins.then_inc(s["qk_pe"].sem, 1)

                def scores(it, v):
                    hb, c = divmod(v, TC)
                    if c == 0:
                        pe.wait_ge(*s["qk_t"](it * 2 * nparts + nparts * (hb + 1)))
                    n = (c + 1) * P
                    x0 = 4 * (hb % 2)
                    q = [X[:, (x0 + i) * S + c * P:(x0 + i) * S + (c + 1) * P] for i in (0, 2)]
                    k = [X[:, (x0 + i) * S:(x0 + i + 1) * S] for i in (1, 3)]
                    if l == 0:
                        pe.wait_ge(*s["logits"](it * 2 * TC + (v - 1 + CREDIT)))
                        for i in range(2):
                            r = slice(i * DH, (i + 1) * DH)
                            ins = pe.matmul(bank[2 + 2 * (v % 2) + i][:, 0:n], q[0][r], k[0][r, 0:n],
                                            start=True, stop=True)
                    else:
                        pe.wait_ge(*s["logits"](it * 2 * TC + (v + CREDIT)))
                        w0 = widths(l, c)[0]
                        for g, (qq, kk, r, k0, w, m0, m1) in enumerate((
                                (q[0], k[0], slice(0, DH), n - w0, w0, 2 * P - w0, 2 * P),
                                (q[0], k[0], slice(DH, P), 0, n, M_4 + S - n, M_4 + S),
                                (q[1], k[1], slice(DH, P), 0, n, M_16 + S - n, M_16 + S))):
                            pe.matmul(bank[2 + g][:, 0:w], qq[r], kk[r, k0:k0 + w], start=True, stop=False)
                            ins = pe.matmul(bank[2 + g][:, 0:w], identb[:, :], maskb[:, m0:m1],
                                            start=False, stop=True)
                    ins.then_inc(s["s_pe"].sem, 1)

                def keys(c):
                    w0 = widths(1, c)[0] // P
                    return [(0, c + 1 - w0 + i) for i in range(w0)] + [(g, i) for g in (1, 2) for i in range(c + 1)]

                def probs_t(it, v):
                    hb, c = divmod(v, TC)
                    if l == 0:
                        pe.wait_ge(*s["probs"](it * 2 * TC + (v + 1)))
                        pe.wait_ge(*s["pt"](it * 2 * TC + v))
                        for i in range(c + 1):
                            at = 2 * (v % 2) * S + i * P
                            ins = pe.transpose(bank[6][:, i * P:(i + 1) * P], W[:, at:at + P], ident)
                        ins.then_inc(s["pt_pe"].sem, 1)
                    else:
                        pe.wait_ge(*s["exps"](it * 2 * TC + (v + 1)))
                        for r in range(ROUNDS[c]):
                            done = hb * HEAD_ROUNDS + ROUND0[c] + r
                            pe.wait_ge(*s["pt"](it * 2 * HEAD_ROUNDS + max(done - 1, 0)))
                            rr = (ROUND0[c] + r) % 2
                            for i in range(4 * r, min(4 * r + 4, len(keys(c)))):
                                at = 1280 * (v % 2) + i * P
                                ins = pe.transpose(bank[5 + rr][:, (i % 4) * P:(i % 4 + 1) * P], W[:, at:at + P], ident)
                            ins.then_inc(s["pt_pe"].sem, 1)

                def values(it, v):
                    hb, c = divmod(v, TC)
                    h = it * 2 + hb
                    pe.wait_ge(*s["o_out"](it * 2 * TC + (v - 1 + CREDIT)))
                    if l == 0:
                        pe.wait_ge(*s["pt"](it * 2 * TC + (v + 1)))
                        for i in range(c + 1):
                            at = 2048 + S * (v % 2) + i * P
                            ins = pe.matmul(bank[O_BANK[v % 2]][:, 0:P], W[:, at:at + P],
                                            val[0][:, i, ds(h * P, P)], start=(i == 0), stop=(i == c))
                    else:
                        pe.wait_ge(*s["pt"](it * 2 * HEAD_ROUNDS + (hb * HEAD_ROUNDS + ROUND0[c] + ROUNDS[c])))
                        for i, (g, kc) in enumerate(keys(c)):
                            ins = pe.matmul(bank[O_BANK[v % 2]][:, 0:DH], W[:, 2560 + i * P:2560 + (i + 1) * P],
                                            val[1][:, kc, ds(h * DH + g * HALF, DH)],
                                            start=(i == 0), stop=(i == len(keys(c)) - 1))
                    ins.then_inc(s["o_pe"].sem, 1)

                def two_heads(it, last=False):
                    for v in range(2 * TC):
                        probs_t(it, v)
                        if v + 2 < 2 * TC or not last:
                            scores(it, v + 2)
                        more = parts_after(l, v) if v // TC == 0 or not last else []
                        for i in more[:1]:
                            part(it, v // TC + 1, i)
                        values(it, v)
                        for i in more[1:]:
                            part(it, v // TC + 1, i)

                for i in range(nparts):
                    part(0, 0, i)
                scores(0, 0)
                scores(0, 1)
                with pe.Fori(0, H // 2 - 1) as it:
                    two_heads(it)
                two_heads(H // 2 - 1, last=True)

                ok = KC if l == 0 else 4
                ow = D if l == 0 else HALF
                o3 = XN[:, 0:TC * ow].rearrange("p (c n) -> p c n", c=TC)
                if l == 0:
                    pe.wait_ge(*s["sub_ready"](TC))
                else:
                    pe.wait_ge(*s["o_out"](CREDIT + TC * H))
                for k in range(ok):
                    if k >= 4:
                        pe.wait_ge(*s["ot_ready"](k - 3))
                    for c in range(TC):
                        ins = pe.transpose(bank[4 + k % 4][:, c * P:(c + 1) * P], o3[:, c, k * P:(k + 1) * P], ident)
                    ins.then_inc(s["ot_pe"].sem, 1)
                pe.wait_ge(*s["ot_ready"](ok))
                for u in range(2 * TC):
                    hf, c = divmod(u, TC)
                    n = AT["wo", l, hf if l == 0 else 0]
                    arrived(pe, n)
                    if u >= 4:
                        pe.wait_ge(*s["y_added"](u - 3))
                    w3 = slot3(n, ok)
                    for k in range(ok):
                        rhs = w3[:, k, :] if l == 0 else w3[:, k, hf * HALF:(hf + 1) * HALF]
                        ins = pe.matmul(bank[u % 4][:, :], ht3[:, k, c * P:(c + 1) * P], rhs,
                                        start=(k == 0), stop=(k == ok - 1))
                    ins.then_inc(s["wo_pe"].sem, 1)
                    if l == 0 and u in mods_after("wo", 2):
                        mod_reduce(mods_after("wo", 2)[u])
                if l == 0:
                    mod_reduce(N_MOD - 1)
                    pe.wait_ge(mod_row, N_MOD)
                pe.wait_ge(*s["xn2"](TC))
                for k in range(KC):
                    if k >= 4:
                        pe.wait_ge(*s["ht2"](k - 3))
                    for c in range(TC):
                        ins = pe.transpose(bank[4 + k % 4][:, c * P:(c + 1) * P], xn3[:, c, k * P:(k + 1) * P], ident)
                    ins.then_inc(s["xt2_pe"].sem, 1)
                pe.wait_ge(*s["ht2"](KC))
                pe.wait_ge(*s["rw_in"](64))
                pe.wait_ge(*s["y_added"](2 * TC))
                for c in range(TC):
                    for k in range(KC):
                        ins = pe.matmul(bank[0][:, c * NR:(c + 1) * NR], ht3[:, k, c * P:(c + 1) * P],
                                        rw3[:, k, :], start=(k == 0), stop=(k == KC - 1))
                ins.then_inc(s["route_pe"].sem, 1)
                pe.wait_ge(*s["picked"](1))
                m3 = W[:, 656:784].rearrange("p (c n) -> p c n", c=TC)
                for c in range(TC):
                    for cc in range(c + 1):
                        pe.matmul(bank[1][:, c * E:(c + 1) * E], tri if cc == c else ones, m3[:, cc, :],
                                  start=(cc == 0), stop=(cc == c))
                for cc in range(TC):
                    ins = pe.matmul(bank[1][:, TC * E:TC * E + E], ones, m3[:, cc, :],
                                    start=(cc == 0), stop=(cc == TC - 1))
                ins.then_inc(s["rank_pe"].sem, 1)
                pe.wait_ge(*s["tab_f"](1))
                for b in range(TC):
                    ins = pe.transpose(bank[2][:, b * E:(b + 1) * E], W[0:E, 2560 + b * P:2560 + (b + 1) * P],
                                       ident[0:E, 0:E])
                ins.then_inc(s["tab_pe"].sem, 1)
                pe.wait_ge(*s["tok_ready"](1))

                m = AT["moe", l, 0]
                pe.sem_inc(s["hid_pe"].sem, CREDIT)

                def rows(e, b, r):
                    if r == 0:
                        pe.wait_ge(*s["gath"][b]((e - b) * 8 + 16))
                    if not (isinstance(e, int) and e == 0 and r == 0):
                        pe.wait_ge(*s["xr_t"](e * 2 + r))
                    for q in range(4):
                        k = 4 * r + q
                        ins = pe.transpose(bank[0][:, q * P:(q + 1) * P], V[:, b * D + k * P:b * D + (k + 1) * P], ident)
                    ins.then_inc(s["xr_pe"].sem, 1)

                def gate_up(e, b, n, turn, between=None):
                    pe.wait_ge(*s["xr_t"](e * 2 + 2))
                    if not (isinstance(e, int) and e < 2):
                        pe.wait_ge(*s["hid"](e - 1))
                    for i in range(2):
                        if i and between:
                            between()
                        arrived(pe, n + i, turn)
                        for k in range(KC):
                            at = 2 * D + b * D + k * P
                            ins = pe.matmul(bank[2 + 2 * i + b][:, :], V[:, at:at + P], slot3(n + i)[:, k, :],
                                            start=(k == 0), stop=(k == KC - 1))
                        ins.then_inc(s["gu_pe"].sem, 1)

                def hidden_t(e, b):
                    pe.wait_ge(*s["hid"](e + 1))
                    if not (isinstance(e, int) and e == 0):
                        pe.wait_ge(*s["hid_t"](e))
                    for k in range(4):
                        at = 4 * D + b * HALF + k * P
                        ins = pe.transpose(bank[1][:, k * P:(k + 1) * P], V[:, at:at + P], ident)
                    ins.then_inc(s["hid_pe"].sem, 1)

                def down(e, b, n, turn, more):
                    if more:
                        rows(e + 2, b, 0)
                    arrived(pe, n, turn)
                    pe.wait_ge(*s["hid_t"](e + 1))
                    if not (isinstance(e, int) and e == 0):
                        pe.wait_ge(*s["y_evac"](e * 2))
                    for hf in range(2):
                        if hf and more:
                            rows(e + 2, b, 1)
                        for k in range(4):
                            at = 5 * D + b * HALF + k * P
                            ins = pe.matmul(bank[6 + hf][:, :], V[:, at:at + P],
                                            slot3(n, 4)[:, k, hf * HALF:(hf + 1) * HALF],
                                            start=(k == 0), stop=(k == 3))
                        ins.then_inc(s["dn_pe"].sem, 1)

                for b in range(2):
                    for r in range(2):
                        rows(b, b, r)
                gate_up(0, 0, m, 0)
                with pe.Fori(0, 15) as it:
                    for b in range(2):
                        e = it * 2 + b
                        gate_up(e + 1, 1 - b, m + 2 + 3 * b, it, lambda: hidden_t(e, b))
                        down(e, b, m + 4 + 3 * b, it, True)
                gate_up(E - 1, 1, m + 92, 0, lambda: hidden_t(E - 2, 0))
                down(E - 2, 0, m + 94, 0, False)
                hidden_t(E - 1, 1)
                down(E - 1, 1, m + 95, 0, False)

                most = pe.value_load(flag[0:1, 0:1], min_val=0, max_val=S)
                with pe.If(most > P):
                    pe.wait_ge(*s["y_evac"](2 * E))
                    for bb in range(1, TC):
                        with pe.Fori(0, E) as e:
                            u0 = (bb - 1) * E
                            pe.wait_ge(*o["g"](e * 16 + (16 * u0 + 16)))
                            for r in range(2):
                                pe.wait_ge(*o["xr_t"](e * 2 + (2 * u0 + r)))
                                for q in range(4):
                                    k = 4 * r + q
                                    ins = pe.transpose(bank[0][:, q * P:(q + 1) * P], V[:, k * P:(k + 1) * P], ident)
                                ins.then_inc(o["xr_pe"].sem, 1)
                            pe.wait_ge(*o["xr_t"](e * 2 + (2 * u0 + 2)))
                            pe.wait_ge(*o["w"](e * 48 + (48 * u0 + 48)))
                            for i in range(2):
                                for k in range(KC):
                                    ins = pe.matmul(bank[2 + 2 * i][:, :], V[:, 2 * D + k * P:2 * D + (k + 1) * P],
                                                    slot3(i)[:, k, :], start=(k == 0), stop=(k == KC - 1))
                                ins.then_inc(o["gu_pe"].sem, 1)
                            pe.wait_ge(*o["hid"](e + (u0 + 1)))
                            for k in range(4):
                                ins = pe.transpose(bank[1][:, k * P:(k + 1) * P],
                                                   V[:, 4 * D + k * P:4 * D + (k + 1) * P], ident)
                            ins.then_inc(o["hid_pe"].sem, 1)
                            pe.wait_ge(*o["hid_t"](e + (u0 + 1)))
                            for hf in range(2):
                                for k in range(4):
                                    ins = pe.matmul(bank[6 + hf][:, :], V[:, 5 * D + k * P:5 * D + (k + 1) * P],
                                                    slot3(2, 4)[:, k, hf * HALF:(hf + 1) * HALF],
                                                    start=(k == 0), stop=(k == 3))
                            ins.then_inc(o["dn_pe"].sem, 1)
                    pe.wait_ge(*o["y"](2 * (TC - 1) * E))


N_VEC = 6 + 4 + 6 + 4
O_BANK = (7, 1)
QK_STEPS = (2, 4)
QK_CREDIT = (4, 8)
STAGE_DMAS = (2 * 16, 8 * 16)
ROUNDS = (1, 2, 2, 3)
ROUND0 = (0, 1, 3, 5)
HEAD_ROUNDS = 8


_INS = ['x', 'c', 'rel_bias', 'ada_w', 'ada_b', 'norm_attn', 'norm_ffn', 'a_w_qkv', 'a_q_norm', 'a_k_norm',
        'a_lambda', 'a_subln', 'a_w_o', 'kv_norm', 'kv_ada_w', 'kv_ada_b', 'kv_w', 'kv_k_norm',
        'b_w_q', 'b_q_norm', 'b_w_o', 'moe_w_group', 'moe_b_group', 'moe_w_expert', 'moe_b_expert',
        'moe_w_gate', 'moe_w_up', 'moe_w_down']


def kernel(**inputs):
    import concourse.bacc as _bacc
    from concourse.bass_utils import run_bass_kernel_spmd as _run

    nc = _bacc.Bacc("TRN2", target_bir_lowering=False, num_devices=1)
    arrays, t = {}, {}

    def declare(name, a):
        arrays[f"in_{name}_dram"] = a
        return nc.dram_tensor(f"in_{name}_dram", a.shape, mybir.dt.from_np(a.dtype), kind="ExternalInput").ap()

    for name in _INS:
        t[name] = declare(name, np.ascontiguousarray(inputs[name]))
    c, m = constants()
    const, masks, buckets = declare("const", c), declare("masks", m), declare("buckets", bucket_table())
    out = nc.dram_tensor("out_0_dram", (1, S, D), F32, kind="ExternalOutput").ap()
    program(nc, t, const, masks, buckets, out)
    r = _run(nc, [arrays], core_ids=[0])
    return r.results[0]["out_0_dram"]
```
